# Optimizing a Trainium2 kernel written in Bass

```python
import numpy as np
import jax
import jax.numpy as jnp
from jax import lax

D_MODEL = 2048
BATCH = 1
SEQ = 256
DEPTH = 1

GLA_HEADS = 4
GLA_DK = D_MODEL // 2
GLA_DV = D_MODEL
GLA_HK = GLA_DK // GLA_HEADS
GLA_HV = GLA_DV // GLA_HEADS
GLA_GATE_RANK = 16
GLA_TAU = 16.0
GLA_CHUNK = 64

NSA_HEADS = 16
NSA_KV_HEADS = 4
NSA_GROUP = NSA_HEADS // NSA_KV_HEADS
NSA_HD = D_MODEL // NSA_HEADS
CMP_STRIDE = 16
CMP_LEN = 2 * CMP_STRIDE
CMP_HIDDEN = 256
SLC_BLOCK = 64
SLC_TOPN = 16
WINDOW = 512
NSA_Q_BLOCK = 32

D_FF = ((8 * D_MODEL // 3 + 255) // 256) * 256

IN_SPLIT_SIZES = (GLA_DK, GLA_DK, GLA_DV, GLA_DV, GLA_GATE_RANK,
                  NSA_HEADS * NSA_HD, 6 * NSA_KV_HEADS * NSA_HD, 3 * NSA_HEADS,
                  2 * D_MODEL)
IN_WIDTH = sum(IN_SPLIT_SIZES)

NEG_INF = -1e30
RMS_EPS = 1e-6

kernel_name = 'hybrid_gla_nsa_block'

def rms_norm(x, g):
    xf = x.astype(jnp.float32)
    y = xf * lax.rsqrt(jnp.mean(xf * xf, axis=-1, keepdims=True) + RMS_EPS)
    return (y * g.astype(jnp.float32)).astype(x.dtype)

def masked_softmax(s, valid):
    s = jnp.where(valid, s.astype(jnp.float32), NEG_INF)
    return jnp.where(valid, jax.nn.softmax(s, axis=-1), 0.0)

def gla_mixer(q, k, v, r, gate_lr, w_gate, b_gate, norm_g):
    B, S, _ = q.shape
    C = GLA_CHUNK
    n = S // C
    H = GLA_HEADS
    f32 = jnp.float32
    log_a = jax.nn.log_sigmoid((gate_lr @ w_gate + b_gate).astype(f32)) / GLA_TAU

    def heads(t, d):
        return t.astype(f32).reshape(B, n, C, H, d).transpose(0, 3, 1, 2, 4)

    qh = heads(q, GLA_HK) * (GLA_HK ** -0.5)
    kh = heads(k, GLA_HK)
    vh = heads(v, GLA_HV)
    b = jnp.cumsum(heads(log_a, GLA_HK), axis=3)
    b_last = b[:, :, :, -1:]
    q_dec = qh * jnp.exp(b)
    k_dec = kh * jnp.exp(-b)
    k_end = kh * jnp.exp(b_last - b)
    causal = jnp.tril(jnp.ones((C, C), dtype=bool))
    attn = jnp.where(causal, jnp.einsum('bhncd,bhnsd->bhncs', q_dec, k_dec), 0.0)
    o_intra = jnp.einsum('bhncs,bhnse->bhnce', attn, vh)

    def step(state, inp):
        q_c, k_c, v_c, decay = inp
        o = jnp.einsum('bhcd,bhde->bhce', q_c, state)
        state = decay[..., None] * state + jnp.einsum('bhcd,bhce->bhde', k_c, v_c)
        return state, o

    xs = (jnp.moveaxis(q_dec, 2, 0), jnp.moveaxis(k_end, 2, 0), jnp.moveaxis(vh, 2, 0),
          jnp.moveaxis(jnp.exp(b_last[:, :, :, 0]), 2, 0))
    state0 = jnp.zeros((B, H, GLA_HK, GLA_HV), f32)
    _, o_inter = lax.scan(step, state0, xs)
    o = o_intra + jnp.moveaxis(o_inter, 0, 2)
    o = o.transpose(0, 2, 3, 1, 4).reshape(B, S, H, GLA_HV)
    o = rms_norm(o, norm_g) * jax.nn.silu(r.astype(f32).reshape(B, S, H, GLA_HV))
    return o.reshape(B, S, GLA_DV).astype(q.dtype)

def compress_blocks(t, pe, w1, w2):
    b, hk, s, hd = t.shape
    chunks = t.reshape(b, hk, s // CMP_STRIDE, CMP_STRIDE, hd)
    blocks = jnp.concatenate([chunks[:, :, :-1], chunks[:, :, 1:]], axis=3) + pe
    flat = blocks.reshape(b, hk, blocks.shape[2], CMP_LEN * hd)
    return jax.nn.silu(flat @ w1) @ w2

def cmp_to_slc_weights(n_cmp, n_slc):
    c0 = np.arange(n_cmp)[:, None] * CMP_STRIDE
    s0 = np.arange(n_slc)[None, :] * SLC_BLOCK
    ov = np.clip(np.minimum(c0 + CMP_LEN, s0 + SLC_BLOCK) - np.maximum(c0, s0), 0, None)
    return jnp.asarray(ov / CMP_LEN, dtype=jnp.float32)

def nsa_mixer(q, kv, gate_logits, pe_k, w_ck1, w_ck2, pe_v, w_cv1, w_cv2):
    B, S, _ = q.shape
    Hk, G, hd, Q = NSA_KV_HEADS, NSA_GROUP, NSA_HD, NSA_Q_BLOCK
    qh = q.reshape(B, S, Hk, G, hd).transpose(0, 2, 3, 1, 4) * (hd ** -0.5)
    kvh = kv.reshape(B, S, 6, Hk, hd).transpose(2, 0, 3, 1, 4)
    k_c_raw, v_c_raw, k_s, v_s, k_w, v_w = (kvh[i] for i in range(6))
    k_cmp = compress_blocks(k_c_raw, pe_k, w_ck1, w_ck2)
    v_cmp = compress_blocks(v_c_raw, pe_v, w_cv1, w_cv2)
    n_cmp = k_cmp.shape[2]
    n_slc = S // SLC_BLOCK
    top_n = min(SLC_TOPN, n_slc)
    m_cs = cmp_to_slc_weights(n_cmp, n_slc)
    cmp_end = jnp.arange(n_cmp) * CMP_STRIDE + CMP_LEN - 1
    blk = jnp.arange(n_slc)
    k_sb = k_s.reshape(B, Hk, n_slc, SLC_BLOCK, hd)
    v_sb = v_s.reshape(B, Hk, n_slc, SLC_BLOCK, hd)
    pad = ((0, 0), (0, 0), (WINDOW, 0), (0, 0))
    k_wp = jnp.pad(k_w, pad)
    v_wp = jnp.pad(v_w, pad)
    gates = jax.nn.sigmoid(gate_logits.astype(jnp.float32)).reshape(B, S, 3, Hk, G).transpose(2, 0, 3, 4, 1)
    gather = jax.vmap(jax.vmap(lambda blocks, idx: blocks[idx]))

    def block(i):
        start = i * Q
        t = start + jnp.arange(Q)
        qb = lax.dynamic_slice_in_dim(qh, start, Q, axis=3)
        s_c = jnp.einsum('bhgqd,bhcd->bhgqc', qb, k_cmp)
        p_c = masked_softmax(s_c, cmp_end[None, :] <= t[:, None])
        o_c = jnp.einsum('bhgqc,bhcd->bhgqd', p_c, v_cmp)
        imp = jnp.einsum('bhgqc,cn->bhqn', p_c, m_cs)
        cur = t[:, None] // SLC_BLOCK
        forced = (blk[None, :] == 0) | (blk[None, :] == cur) | (blk[None, :] == cur - 1)
        imp = jnp.where(forced, jnp.inf, imp)
        imp = jnp.where(blk[None, :] * SLC_BLOCK <= t[:, None], imp, -jnp.inf)
        _, idx = lax.top_k(imp, top_n)
        k_sel = gather(k_sb, idx)
        v_sel = gather(v_sb, idx)
        pos = idx[..., None] * SLC_BLOCK + jnp.arange(SLC_BLOCK)
        valid_sel = (pos <= t[:, None, None])[:, :, None].reshape(B, Hk, 1, Q, top_n * SLC_BLOCK)
        s_s = jnp.einsum('bhgqd,bhqnkd->bhgqnk', qb, k_sel).reshape(B, Hk, G, Q, top_n * SLC_BLOCK)
        p_s = masked_softmax(s_s, valid_sel)
        o_s = jnp.einsum('bhgqm,bhqmd->bhgqd', p_s, v_sel.reshape(B, Hk, Q, top_n * SLC_BLOCK, hd))
        k_win = lax.dynamic_slice_in_dim(k_wp, start, Q + WINDOW, axis=2)
        v_win = lax.dynamic_slice_in_dim(v_wp, start, Q + WINDOW, axis=2)
        kpos = start - WINDOW + jnp.arange(Q + WINDOW)
        valid_w = (kpos[None, :] <= t[:, None]) & (kpos[None, :] > t[:, None] - WINDOW) & (kpos[None, :] >= 0)
        s_w = jnp.einsum('bhgqd,bhkd->bhgqk', qb, k_win)
        p_w = masked_softmax(s_w, valid_w)
        o_w = jnp.einsum('bhgqk,bhkd->bhgqd', p_w, v_win)
        gb = lax.dynamic_slice_in_dim(gates, start, Q, axis=4)[..., None]
        return gb[0] * o_c + gb[1] * o_s + gb[2] * o_w

    out = lax.map(block, jnp.arange(S // Q))
    out = out.transpose(1, 0, 4, 2, 3, 5).reshape(B, S, NSA_HEADS * hd)
    return out.astype(q.dtype)

def setup_inputs(seed: int = 0) -> dict:
    key = jax.random.key(seed)
    ks = jax.random.split(key, 24)
    L = DEPTH
    f32 = jnp.float32

    def nrm(k, shape, fan_in):
        return jax.random.normal(k, shape, f32) * (fan_in ** -0.5)

    def gain(k, shape):
        return 1.0 + 0.02 * jax.random.normal(k, shape, f32)

    cin = CMP_LEN * NSA_HD
    return {
        'x': jax.random.normal(ks[0], (BATCH, SEQ, D_MODEL), f32),
        'g_mix': gain(ks[1], (L, D_MODEL)),
        'w_in': nrm(ks[2], (L, D_MODEL, IN_WIDTH), D_MODEL),
        'w_gla_gate': nrm(ks[3], (L, GLA_GATE_RANK, GLA_DK), GLA_GATE_RANK),
        'b_gla_gate': 0.1 * jax.random.normal(ks[4], (L, GLA_DK), f32),
        'g_gla_out': gain(ks[5], (L, GLA_HV)),
        'pe_cmp_k': 0.1 * jax.random.normal(ks[6], (L, CMP_LEN, NSA_HD), f32),
        'w_cmp_k1': nrm(ks[7], (L, cin, CMP_HIDDEN), cin),
        'w_cmp_k2': nrm(ks[8], (L, CMP_HIDDEN, NSA_HD), CMP_HIDDEN),
        'pe_cmp_v': 0.1 * jax.random.normal(ks[9], (L, CMP_LEN, NSA_HD), f32),
        'w_cmp_v1': nrm(ks[10], (L, cin, CMP_HIDDEN), cin),
        'w_cmp_v2': nrm(ks[11], (L, CMP_HIDDEN, NSA_HD), CMP_HIDDEN),
        'w_proj_gla': nrm(ks[12], (L, GLA_DV, D_MODEL), GLA_DV),
        'w_proj_nsa': nrm(ks[13], (L, NSA_HEADS * NSA_HD, D_MODEL), NSA_HEADS * NSA_HD),
        'w_out': nrm(ks[14], (L, D_MODEL, D_MODEL), D_MODEL),
        'g_ffn': gain(ks[15], (L, D_MODEL)),
        'w_ffn_gate': nrm(ks[16], (L, D_MODEL, D_FF), D_MODEL),
        'w_ffn_up': nrm(ks[17], (L, D_MODEL, D_FF), D_MODEL),
        'w_ffn_down': nrm(ks[18], (L, D_FF, D_MODEL), D_FF),
        'g_final': gain(ks[19], (D_MODEL,)),
    }

def reference(x, g_mix, w_in, w_gla_gate, b_gla_gate, g_gla_out, pe_cmp_k, w_cmp_k1, w_cmp_k2,
              pe_cmp_v, w_cmp_v1, w_cmp_v2, w_proj_gla, w_proj_nsa, w_out, g_ffn,
              w_ffn_gate, w_ffn_up, w_ffn_down, g_final):
    split_points = [int(v) for v in np.cumsum(IN_SPLIT_SIZES)[:-1]]
    for l in range(DEPTH):
        h = rms_norm(x, g_mix[l])
        z = h @ w_in[l]
        gq, gk, gv, gr, glr, nq, nkv, ngate, mgate = jnp.split(z, split_points, axis=-1)
        o_gla = gla_mixer(gq, gk, gv, gr, glr, w_gla_gate[l], b_gla_gate[l], g_gla_out[l])
        o_nsa = nsa_mixer(nq, nkv, ngate, pe_cmp_k[l], w_cmp_k1[l], w_cmp_k2[l],
                          pe_cmp_v[l], w_cmp_v1[l], w_cmp_v2[l])
        gate_a, gate_b = jnp.split(jax.nn.sigmoid(mgate), 2, axis=-1)
        merged = gate_a * (o_gla @ w_proj_gla[l]) + gate_b * (o_nsa @ w_proj_nsa[l])
        x = x + merged @ w_out[l]
        h = rms_norm(x, g_ffn[l])
        x = x + (jax.nn.silu(h @ w_ffn_gate[l]) * (h @ w_ffn_up[l])) @ w_ffn_down[l]
    return rms_norm(x, g_final)


_drawn_inputs = setup_inputs


def setup_inputs(seed=0):
    import zlib

    import numpy as np

    out = dict(_drawn_inputs(seed))
    spreads = {}
    factors = {'g_mix': 3.653,
     'b_gla_gate': 3.927,
     'g_gla_out': 8.0,
     'pe_cmp_k': 23.838,
     'pe_cmp_v': 25.093,
     'g_ffn': 11.899,
     'g_final': 8.485}
    for name, (base, spread) in spreads.items():
        noise = np.random.default_rng([zlib.crc32(name.encode()), seed]).standard_normal(out[name].shape)
        drawn = base * np.exp(spread * noise) if base else spread * noise
        out[name] = jnp.asarray(drawn.astype(out[name].dtype))
    for name, factor in factors.items():
        out[name] = (out[name] * factor).astype(out[name].dtype)
    return out
```

```python
from contextlib import ExitStack, contextmanager

import numpy as np

import concourse.bass as bass
from concourse import mybir

F32 = mybir.dt.float32
F32R = mybir.dt.float32r
I32 = mybir.dt.int32
ALU = mybir.AluOpType
ACT = mybir.ActivationFunctionType
AX = mybir.AxisListType

P = 128
SEQ = 256
NT = SEQ // P
D = 2048
KT = D // P
COL = 512
D_FF = 5632
KT_FF = D_FF // P

GLA_HEADS, GLA_DK, GLA_DV, GATE_RANK, CHUNK, TAU = 4, 1024, 2048, 16, 64, 16.0
HK, HV = GLA_DK // GLA_HEADS, GLA_DV // GLA_HEADS
FT = HK // P
NCH = SEQ // CHUNK
HEADS, KV_HEADS, HD = 16, 4, 128
GROUP = HEADS // KV_HEADS
STRIDE, CMP_LEN, CMP_HIDDEN = 16, 32, 256
NCMP = SEQ // STRIDE - 1
NC4 = KV_HEADS * NCMP
EPS = 1e-6
NEG = -1e30

O_GQ = 0
O_GK = O_GQ + GLA_DK
O_GV = O_GK + GLA_DK
O_GR = O_GV + GLA_DV
O_LR = O_GR + GLA_DV
O_NQ = O_LR + GATE_RANK
O_KV = O_NQ + HEADS * HD
O_NG = O_KV + 6 * KV_HEADS * HD
O_MG = O_NG + 3 * HEADS
IN_WIDTH = O_MG + 2 * D
NSMALL = GATE_RANK + 3 * HEADS

SB = 1024
KSB = SB // COL
SLOTS = 4
LEAD = 3
NCOL = KT // KSB
NDOWN = KT_FF // KSB
NCB = 8
FFB = D_FF // COL
STREAM = 30 * NCOL + 2 * NCB + 3 * 4 * NCOL + 2 * FFB * NCOL + 4 * NDOWN

C_GMIX, C_GFFN, C_BG, C_PEK, C_PEV = 0, KT, 2 * KT, 2 * KT + GLA_DK // P, 2 * KT + GLA_DK // P + CMP_LEN
NPAR = C_PEV + CMP_LEN


class Tally:

    def __init__(self, sem):
        self.sem, self.n, self.i, self.per = sem, 0, None, 0

    def more(self, k=1):
        self.n += k
        return self.now()

    def now(self, back=0):
        if self.i is None or self.per == 0:
            return self.n - back
        return self.i * self.per + (self.n - back)


class Counts:

    def __init__(self, sems):
        self.all = {n: Tally(s) for n, s in sems.items()}

    def __getattr__(self, name):
        return self.all[name]

    def __getitem__(self, name):
        return self.all[name]

    @contextmanager
    def loop(self, eng, trips, **pers):
        before = {n: t.n for n, t in self.all.items()}
        with eng.Fori(0, trips) as i:
            for n, t in self.all.items():
                t.i, t.per = i, pers.get(n, 0)
            yield i
        for n, t in self.all.items():
            assert t.n - before[n] == t.per, (n, t.n - before[n], t.per)
            t.n = before[n] + t.per * trips
            t.i, t.per = None, 0


def build(nc, wstream, x, params, wsmall, w_gate, w2, g_gla, g_final, out):
    with ExitStack() as ctx:
        base = [16512]

        def at(name, shape, dt, offset):
            return nc.alloc_sbuf_tensor_at(name, list(shape), dt, offset=offset)

        def region(size):
            r = base[0]
            base[0] += -(-size // 32) * 32
            return r

        def sb(name, shape, dt=F32):
            return at(name, shape, dt, region(4 * int(np.prod(shape[1:]))))

        K = 1024
        ident = sb("ident", [P, P])
        causal_bias = sb("causal_bias", [P, SEQ])
        gla_valid = sb("gla_valid", [P, P])
        cmp_bias = sb("cmp_bias", [P, NT, STRIDE])
        cmp_valid = sb("cmp_valid", [P, NT, STRIDE])
        par = sb("par", [P, NPAR])
        staging = sb("staging", [P, NT, COL])
        z_small = sb("z_small", [P, NT, NSMALL])
        branch_gate = sb("branch_gate", [P, NT, 3, HEADS])
        k_cmp_T = sb("k_cmp_T", [P, NC4])
        v_cmp = sb("v_cmp", [NCMP, KV_HEADS, HD])
        sumsq = sb("sumsq", [P, NT, 4])
        ms = sb("ms", [P, NT])
        rs = sb("rs", [P, NT])
        rs_t = sb("rs_t", [P, NT])
        max_c = sb("max_c", [P, GROUP, NT])
        coef_c = sb("coef_c", [P, GROUP, NT])
        nmax = sb("nmax", [P, NT, 2])
        coef = sb("coef", [P, NT, 2])
        RS = region(5 * K)
        attn_sb = at("attn_sb", [P, 3, P], F32, RS)
        g_gla_bc = at("g_gla_bc", [P, HV], F32, RS + 1536)
        q2 = at("q2", [P, FT, 2, CHUNK], F32, RS + 3584)
        q3 = at("q3", [P, FT, CHUNK], F32, RS + 4608)
        ffn_gate = at("ffn_gate", [P, NT, COL], F32, RS)

        w_raw = [sb(f"w_raw{s}", [P, SB]) for s in range(SLOTS)]
        w_hi = [sb(f"w_hi{s}", [P, SB], F32R) for s in range(SLOTS)]
        w_lo = [sb(f"w_lo{s}", [P, SB], F32R) for s in range(SLOTS)]
        RA, RB, RG, RV, RR, RN, RX = (region(s * K) for s in (32, 16, 32, 16, 16, 16, 16))
        assert base[0] <= nc.sbuf_usable_end, (base[0], nc.sbuf_usable_end)

        h_hi = at("h_hi", [P, KT, SEQ], F32R, RA)
        h_lo = at("h_lo", [P, KT, SEQ], F32R, RA + 16 * K)
        f_hi = at("f_hi", [P, KT, SEQ], F32R, RA)
        f_lo = at("f_lo", [P, KT, SEQ], F32R, RA + 16 * K)
        x_tok = at("x_tok", [P, NT, D], F32, RV)
        square_junk = at("square_junk", [P, D], F32, RG + 16 * K)
        ws_raw = at("ws_raw", [P, KT, NSMALL], F32, RG)
        ws_hi = at("ws_hi", [P, KT, NSMALL], F32R, RG + 4 * K)
        ws_lo = at("ws_lo", [P, KT, NSMALL], F32R, RG + 8 * K)
        w2_sb = at("w2_sb", [P, 2, 2, HD], F32, RN)
        w_gate_sb = at("w_gate_sb", [GATE_RANK, GLA_DK], F32, RN + 2 * K)
        hid = at("hid", [NC4, 2, CMP_HIDDEN], F32, RN + 6 * K)
        hid_e = at("hid_e", [NC4, 2, CMP_HIDDEN], F32, RN + 8 * K)
        hid_T = at("hid_T", [P, 4, 64], F32, RN + 10 * K)
        glr_T = at("glr_T", [GATE_RANK, SEQ], F32, RN + 12 * K)
        ksw_T = at("ksw_T", [P, 2, KV_HEADS, SEQ], F32, RX)
        vsw = at("vsw", [P, 2, NT, COL], F32, RX + 8 * K)
        nq_T = at("nq_T", [P, KV_HEADS, GROUP, SEQ], F32, RN)
        on_T = at("on_T", [P, KV_HEADS, GROUP, SEQ], F32, RN)
        kvc_T = at("kvc_T", [P, 2, KV_HEADS, SEQ], F32, RG)
        flat_at = (RG + 8 * K, RV)
        flat = [at(f"flat{n}", [P, CMP_LEN, KV_HEADS, NCMP], F32, r) for n, r in enumerate(flat_at)]
        flat_hi = [at(f"flat_hi{n}", [P, CMP_LEN, NC4], F32R, r + 7680) for n, r in enumerate(flat_at)]
        flat_lo = [at(f"flat_lo{n}", [P, CMP_LEN, NC4], F32R, r + 15360) for n, r in enumerate(flat_at)]
        gqk_T = at("gqk_T", [P, 2, GLA_HEADS, FT, SEQ], F32, RG)
        decay_sum = at("decay_sum", [P, GLA_HEADS, FT * NCH, CHUNK], F32, RG + 16 * K)
        log_a = at("log_a", [P, GLA_HEADS * FT * SEQ], F32, RV)
        chunk_keep = at("chunk_keep", [P, GLA_HEADS * FT * SEQ], F32, RR)
        e_pos = at("e_pos", [P, FT, NCH, CHUNK], F32, RG + 24 * K)
        e_neg = at("e_neg", [P, FT, NCH, CHUNK], F32, RG + 26 * K)
        e_end = at("e_end", [P, FT, NCH, CHUNK], F32, RG + 28 * K)
        q_dec = at("q_dec", [P, FT, NCH, CHUNK], F32, RG + 30 * K)
        gv = at("gv", [P, GLA_HEADS, NT, COL], F32, RV)
        gr = at("gr", [P, GLA_HEADS, NT, COL], F32, RR)
        og_T = at("og_T", [P, GLA_HEADS, 4, SEQ], F32, RB)
        r_gate = [at(f"r_gate{n}", [P, NT, COL], F32, RB + 4 * K * n) for n in range(2)]
        og_hi = at("og_hi", [P, KT, SEQ], F32R, RV)
        og_lo = at("og_lo", [P, KT, SEQ], F32R, RB)
        merged = at("merged", [P, 4, NT, COL], F32, RR)
        q_st = at("q_st", [P, GROUP, SEQ], F32, RG)
        v_st = at("v_st", [P, 2, NT, HD], F32, RG + 4 * K)
        vc_st = at("vc_st", [NCMP, HD], F32, RG + 6 * K)
        p_T = at("p_T", [P, 2, COL], F32, RG + 7 * K)
        p_sc = at("p_sc", [P, 3 * SEQ], F32, RG + 11 * K)
        p_c = at("p_c", [P, GROUP, NT, STRIDE], F32, RG + 14 * K)
        gate = at("gate", [P, NT, COL], F32, RG + 16 * K)
        on_hi = at("on_hi", [P, KT, SEQ], F32R, RV)
        on_lo = at("on_lo", [P, KT, SEQ], F32R, RB)
        m_hi = at("m_hi", [P, KT, SEQ], F32R, RG)
        m_lo = at("m_lo", [P, KT, SEQ], F32R, RN)
        x1 = at("x1", [P, NT, D], F32, RX)
        act_hi = at("act_hi", [P, KT_FF, SEQ], F32R, RB)
        act_lo = at("act_lo", [P, KT_FF, SEQ], F32R, RB + 44 * K)
        g_fin_bc = at("g_fin_bc", [P, D], F32, RB + 88 * K)

        banks = [ctx.enter_context(nc.psum_tensor(f"bank{n}", [P, COL], F32)) for n in range(8)]
        acc = [banks[0:2], banks[2:4]]
        tp = banks[4:6]
        mix = banks[6:8]

        names = """x_landed0 x_landed1 small_landed xres_landed gfin_landed out_stored
            raw_landed0 raw_landed1 raw_landed2 raw_landed3 hi_ready lo_ready block_done
            acc_free0 acc_free1 tp_ready0 tp_ready1 tp_free0 tp_free1 tp_hi staging_full
            const_step const_ready dve_step act_step sumsq_ready ms_ready rs_guess rs_ready h_tok_ready
            ws_hi_ready ws_lo_ready small_ready z_small_ready branch_e glr_ready glr_T_ready
            flat_ready flat_hi_ready flat_lo_ready hid_e_ready hid_sb_ready hid_tp hid_T_ready cmp_out cmp_sb
            gate_mm gate_sb nega_ready ln_ready gr_e decay_ready exp_ready gla_ops gla_attn attn_ready gla_o_ready
            og_hi_ready og_lo_ready q_st_ready v_st_ready cs_ready cs_sub cs_exp qk_ready nmax_ready
            p_exp p_ready pv_ready on_ready gate_e on_hi_ready on_lo_ready y_ready""".split()
        S = {n: ctx.enter_context(nc.semaphore(n)) for n in names}
        block = ctx.enter_context(nc.Block())

        def f32(ap):
            return ap.bitcast(F32)

        def blocks_of(t):
            return t[:, :, :].rearrange("p (a f) s -> p a f s", f=4)

        gqk_blocks = gqk_T[:, :, :, :, :].rearrange("p n (a b) f s -> p (n a) (b f) s", b=2)

        @block.sync
        def _(sp):
            for s in range(SLOTS):
                sp.dma_start(w_raw[s][:, :], wstream[s]).then_inc(S[f"raw_landed{s}"], 16)
            with sp.Fori(1, STREAM // SLOTS) as i:
                for s in range(SLOTS):
                    sp.wait_ge(S["lo_ready"], i * SLOTS + (s - SLOTS + 1))
                    sp.dma_start(w_raw[s][:, :], wstream[i * SLOTS + s]).then_inc(S[f"raw_landed{s}"], 16)
            for t in range(NT):
                sp.wait_ge(S["y_ready"], t + 1)
                sp.dma_start(out[t], x1[:, t, :]).then_inc(S["out_stored"], 16)
            sp.wait_ge(S["out_stored"], 16 * NT)

        @block.gpsimd
        def _(pool):
            for m, v in ((ident[:, :], 0.0), (causal_bias[:, :], 0.0), (gla_valid[:, :], 1.0),
                         (cmp_bias[:, :, :], 0.0), (cmp_valid[:, :, :], 1.0), (attn_sb[:, :, :], 0.0)):
                nc.gpsimd.memset(m, v).then_inc(S["const_step"], 1)
            pool.wait_ge(S["const_step"], 6)
            diagonal = causal_bias[:, P:SEQ]
            for m, op, fill, start, pattern, per_row in (
                    (ident[:, :], ALU.not_equal, 1.0, 0, [[-1, P]], 1),
                    (diagonal, ALU.is_ge, NEG, 0, [[-1, P]], 1),
                    (gla_valid[:, :], ALU.is_ge, 0.0, 0, [[1, P]], -1),
                    (cmp_bias[:, :, :], ALU.is_ge, NEG, 1 - CMP_LEN, [[P, NT], [-STRIDE, STRIDE]], 1),
                    (cmp_valid[:, :, :], ALU.is_ge, 0.0, 1 - CMP_LEN, [[P, NT], [-STRIDE, STRIDE]], 1)):
                nc.gpsimd.affine_select(out=m, in_=m, compare_op=op, fill=fill, base=start, pattern=pattern,
                                        channel_multiplier=per_row).then_inc(S["const_ready"], 1)

        @block.tensor
        def _(pe):
            c = Counts(S)

            def block_products(j, kts, width, hi, lo, outs, rows, last):
                s = c.lo_ready.n % SLOTS
                pe.wait_ge(S["lo_ready"], c.lo_ready.more())
                for kk in range(kts):
                    k = j * kts + kk
                    wh = w_hi[s][:, kk * width:(kk + 1) * width]
                    wl = w_lo[s][:, kk * width:(kk + 1) * width]
                    for t in range(len(outs)):
                        rows_t = slice(t * P, t * P + rows)
                        nc.tensor.matmul(outs[t], hi[:, k, rows_t], wh, start=k == 0, stop=False)
                        nc.tensor.matmul(outs[t], hi[:, k, rows_t], wl, start=False, stop=False)
                        end = nc.tensor.matmul(outs[t], lo[:, k, rows_t], wh, start=False, stop=k == last)
                end.then_inc(S["block_done"], 1)

            def column(pair, hi, lo, n=NCOL, hooks={}):
                free = c[f"acc_free{pair}"]
                if free.n:
                    pe.wait_ge(free.sem, free.now())
                outs = [acc[pair][t][:, :] for t in range(NT)]
                for j in range(n):
                    block_products(j, KSB, COL, hi, lo, outs, P, n * KSB - 1)
                    for hook in hooks.get(j, ()):
                        hook()

            def tp_wait():
                for b in range(2):
                    free = c[f"tp_free{b}"]
                    if free.n:
                        pe.wait_ge(free.sem, free.now())
                    free.more()

            def tp_settled():
                for b in range(2):
                    pe.wait_ge(S[f"tp_free{b}"], c[f"tp_free{b}"].now())

            def transpose_staging():
                pe.wait_ge(S["staging_full"], c.staging_full.more(2))
                tp_wait()
                for b in range(2):
                    for f in range(2):
                        for t in range(NT):
                            end = nc.tensor.transpose(
                                tp[b][:, f * SEQ + t * P:f * SEQ + (t + 1) * P],
                                staging[:, t, (2 * b + f) * P:(2 * b + f + 1) * P], ident[:, :])
                    end.then_inc(S[f"tp_ready{b}"], 1)

            pe.wait_ge(S["const_ready"], 5)
            pe.wait_ge(S["h_tok_ready"], NT)
            for f in range(KT // 4):
                tp_wait()
                for b in range(2):
                    for kk in range(2):
                        k = 4 * f + 2 * b + kk
                        for t in range(NT):
                            end = nc.tensor.transpose(tp[b][:, kk * SEQ + t * P:kk * SEQ + (t + 1) * P],
                                                      x_tok[:, t, k * P:(k + 1) * P], ident[:, :])
                    end.then_inc(S[f"tp_ready{b}"], 1)
            tp_settled()
            pe.wait_ge(S["ws_lo_ready"], 1)
            for t in range(NT):
                rows = slice(t * P, (t + 1) * P)
                o = mix[0][:, t * NSMALL:(t + 1) * NSMALL]
                for k in range(KT):
                    nc.tensor.matmul(o, h_hi[:, k, rows], ws_hi[:, k, :], start=k == 0, stop=False)
                    nc.tensor.matmul(o, h_hi[:, k, rows], ws_lo[:, k, :], start=False, stop=False)
                    end = nc.tensor.matmul(o, h_lo[:, k, rows], ws_hi[:, k, :], start=False, stop=k == KT - 1)
            end.then_inc(S["small_ready"], 1)

            def feature_major(trips, hooks=lambda i: {}, **more):
                pers = dict(lo_ready=NCOL, tp_free0=1, tp_free1=1, staging_full=2)
                pers.update(more)
                with c.loop(pe, trips, **pers) as i:
                    column(0, h_hi, h_lo, hooks=hooks(i))
                    transpose_staging()

            def token_major(trips):
                with c.loop(pe, trips, lo_ready=2 * NCOL, acc_free0=2, acc_free1=2):
                    for pair in range(2):
                        column(pair, h_hi, h_lo)
                        c[f"acc_free{pair}"].more(2)

            feature_major(2)
            pe.wait_ge(S["z_small_ready"], 1)
            for t in range(NT):
                end = nc.tensor.transpose(mix[1][0:GATE_RANK, t * P:(t + 1) * P],
                                          z_small[:, t, 0:GATE_RANK], ident[:, :])
            end.then_inc(S["glr_ready"], 1)
            feature_major(2)
            for pair in range(2):
                column(pair, h_hi, h_lo)
                c[f"acc_free{pair}"].more(2)

            pe.wait_ge(S["acc_free1"], c.acc_free1.now())
            for n in range(2):
                pe.wait_ge(S["flat_lo_ready"], n + 1)
                for j in range(NCB):
                    block_products(j, 4, CMP_HIDDEN, flat_hi[n], flat_lo[n],
                                   [acc[1][n][0:NC4, 0:CMP_HIDDEN]], NC4, CMP_LEN - 1)
            pe.wait_ge(S["hid_sb_ready"], 1)
            for n in range(2):
                for k in range(2):
                    end = nc.tensor.transpose(mix[0][:, (2 * n + k) * 64:(2 * n + k) * 64 + NC4],
                                              hid[:, n, k * P:(k + 1) * P], ident[0:NC4, 0:NC4])
            end.then_inc(S["hid_tp"], 1)
            pe.wait_ge(S["hid_T_ready"], 1)
            for k in range(2):
                nc.tensor.matmul(mix[1][:, 0:NC4], w2_sb[:, 0, k, :], hid_T[:, k, 0:NC4],
                                 start=k == 0, stop=k == 1)
            for g in range(KV_HEADS):
                for k in range(2):
                    end = nc.tensor.matmul(mix[0][0:NCMP, g * HD:(g + 1) * HD],
                                           hid_T[:, 2 + k, g * NCMP:(g + 1) * NCMP], w2_sb[:, 1, k, :],
                                           start=k == 0, stop=k == 1)
            end.then_inc(S["cmp_out"], 1)

            pe.wait_ge(S["cmp_sb"], 2)
            pe.wait_ge(S["glr_T_ready"], 1)
            gate_banks = [acc[1][0], acc[1][1], mix[0], mix[1]]
            for f in range(GLA_DK // P):
                end = nc.tensor.matmul(gate_banks[f // 2][:, (f % 2) * SEQ:(f % 2 + 1) * SEQ],
                                       w_gate_sb[:, f * P:(f + 1) * P], glr_T[:, :], start=True, stop=True)
            end.then_inc(S["gate_mm"], 1)

            feature_major(2)
            feature_major(2)
            pe.wait_ge(S["gate_sb"], GLA_DK // P)
            token_major(2)
            token_major(2)

            def gla_scores():
                pe.wait_ge(S["gla_ops"], c.gla_ops.more())
                for tile, kc, qc in ((0, 0, 0), (0, 0, 1), (0, 1, 1), (1, 0, 2), (1, 0, 3), (1, 1, 2),
                                     (1, 1, 3), (2, 2, 2), (2, 2, 3), (2, 3, 3)):
                    row = (kc % 2) * CHUNK
                    col = tile * P + (qc % 2) * CHUNK
                    o = mix[0][row:row + CHUNK, col:col + CHUNK]
                    for f in range(FT):
                        keys = (e_neg if kc == qc else e_end)[:, f, kc, :]
                        queries = (q_dec[:, f, qc, :] if qc - kc <= 1 else
                                   q2[:, f, qc - 2, :] if qc - kc == 2 else q3[:, f, :])
                        end = nc.tensor.matmul(o, keys, queries, start=f == 0, stop=f == FT - 1)
                end.then_inc(S["gla_attn"], 1)

            def gla_values(i):
                def go():
                    pe.wait_ge(S["attn_ready"], c.attn_ready.more())
                    pe.wait_ge(S["acc_free1"], c.acc_free1.now())
                    nc.tensor.matmul(acc[1][0][:, :], attn_sb[:, 0, :], gv[:, i, 0, :], start=True, stop=True)
                    nc.tensor.matmul(acc[1][1][:, :], attn_sb[:, 1, :], gv[:, i, 0, :], start=True, stop=False)
                    nc.tensor.matmul(acc[1][1][:, :], attn_sb[:, 2, :], gv[:, i, 1, :], start=False,
                                     stop=True).then_inc(S["gla_o_ready"], 1)
                return go

            feature_major(GLA_HEADS, lambda i: {2: [gla_scores], 3: [gla_values(i)], 5: [transpose_staging]},
                          gla_ops=1, attn_ready=1, tp_free0=2, tp_free1=2, staging_full=4)

            def cmp_scores(i):
                def go():
                    pe.wait_ge(S["q_st_ready"], c.q_st_ready.more())
                    pe.wait_ge(S["v_st_ready"], c.v_st_ready.more())
                    tp_settled()
                    for u in range(GROUP):
                        for t in range(NT):
                            at_col = (u * NT + t) * STRIDE
                            end = nc.tensor.matmul(tp[1][:, at_col:at_col + NCMP], q_st[:, u, t * P:(t + 1) * P],
                                                   k_cmp_T[:, bass.ds(i * NCMP, NCMP)], start=True, stop=True)
                    end.then_inc(S["cs_ready"], 1)
                return go

            def scores(i, u):
                def go():
                    nc.tensor.matmul(mix[0][:, 0:SEQ], q_st[:, u, 0:P], ksw_T[:, :, i, 0:P],
                                     start=True, stop=True)
                    nc.tensor.matmul(mix[1][:, :], q_st[:, u, P:SEQ], ksw_T[:, :, i, :], start=True,
                                     stop=True).then_inc(S["qk_ready"], 1)
                return go

            def probs_T(u):
                def go():
                    pe.wait_ge(S["p_ready"], c.p_ready.more())
                    if u:
                        pe.wait_ge(S["on_ready"], c.on_ready.now())
                    tp_wait()
                    for n in range(2):
                        nc.tensor.transpose(tp[n][:, 0:P], p_sc[:, n * P:(n + 1) * P], ident[:, :])
                        for k in range(NT):
                            off = SEQ + n * SEQ + k * P
                            nc.tensor.transpose(tp[n][:, (1 + k) * P:(2 + k) * P], p_sc[:, off:off + P],
                                                ident[:, :])
                        nc.tensor.transpose(tp[n][0:NCMP, 3 * P:4 * P], p_c[:, u, n, 0:NCMP],
                                            ident[:, :]).then_inc(S[f"tp_ready{n}"], 1)
                return go

            def outputs(u):
                def go():
                    tp_settled()
                    c.on_ready.more()
                    o, late = tp[0][:, 0:SEQ], tp[0][:, P:SEQ]
                    nc.tensor.matmul(o, v_st[:, 0, 0, :], p_T[:, 0, 0:SEQ], start=True, stop=False)
                    nc.tensor.matmul(o, v_st[:, 1, 0, :], p_T[:, 1, 0:SEQ], start=False, stop=False)
                    nc.tensor.matmul(o, vc_st[:, :], p_T[0:NCMP, :, SEQ + P:2 * SEQ], start=False, stop=False)
                    nc.tensor.matmul(late, v_st[:, 0, 1, :], p_T[:, 0, SEQ:SEQ + P], start=False, stop=False)
                    nc.tensor.matmul(late, v_st[:, 1, 1, :], p_T[:, 1, SEQ:SEQ + P], start=False,
                                     stop=True).then_inc(S["pv_ready"], 1)
                return go

            with c.loop(pe, KV_HEADS, lo_ready=2 * NCOL, acc_free0=2, acc_free1=2, tp_free0=4, tp_free1=4,
                        q_st_ready=1, v_st_ready=1, on_ready=4, p_ready=4) as i:
                column(0, h_hi, h_lo, hooks={0: [cmp_scores(i), scores(i, 0)], 3: [probs_T(0), scores(i, 1)],
                                             4: [outputs(0)], 6: [probs_T(1), scores(i, 2)], 7: [outputs(1)]})
                c.acc_free0.more(2)
                pe.wait_ge(S["og_lo_ready"], 4)
                column(1, og_hi, og_lo, hooks={1: [probs_T(2), scores(i, 3)], 2: [outputs(2)],
                                               5: [probs_T(3)], 6: [outputs(3)]})
                c.acc_free1.more(2)
                pe.wait_ge(S["on_ready"], c.on_ready.now())

            with c.loop(pe, 4, lo_ready=2 * NCOL, acc_free0=2, acc_free1=2, tp_free0=1, tp_free1=1,
                        staging_full=2):
                column(0, h_hi, h_lo)
                c.acc_free0.more(2)
                pe.wait_ge(S["on_lo_ready"], 4)
                column(1, on_hi, on_lo)
                c.acc_free1.more(2)
                transpose_staging()
            tp_settled()

            with c.loop(pe, 4, lo_ready=NCOL, tp_free0=1, tp_free1=1, staging_full=2):
                column(0, m_hi, m_lo)
                transpose_staging()
            tp_settled()

            with c.loop(pe, FFB, lo_ready=2 * NCOL, acc_free0=2, tp_free0=1, tp_free1=1, staging_full=2):
                column(0, f_hi, f_lo)
                c.acc_free0.more(2)
                column(1, f_hi, f_lo)
                transpose_staging()
            tp_settled()
            with c.loop(pe, 2, lo_ready=2 * NDOWN, acc_free0=2, acc_free1=2):
                for pair in range(2):
                    column(pair, act_hi, act_lo, n=NDOWN)
                    c[f"acc_free{pair}"].more(2)

        SPLITS = {n: 16 * NCOL // SLOTS for n in ("raw_landed0", "raw_landed1", "raw_landed2", "raw_landed3")}

        @block.scalar
        def _(act):
            c = Counts(S)
            LOOP = dict(SPLITS, hi_ready=NCOL, block_done=NCOL)
            LOOP2 = {n: 2 * v for n, v in LOOP.items()}

            def split():
                s = c.hi_ready.n % SLOTS
                landed = c[f"raw_landed{s}"]
                act.wait_ge(landed.sem, landed.more(16))
                c.hi_ready.more()
                if c.hi_ready.n > SLOTS:
                    act.wait_ge(S["block_done"], c.hi_ready.now(SLOTS))
                nc.scalar.activation(w_hi[s][:, :], w_raw[s][:, :], ACT.Copy).then_inc(S["hi_ready"], 1)

            def blocks(n=NCOL, hooks={}, splits=None):
                for j in range(n):
                    if splits is None or j < splits:
                        split()
                    for hook in hooks.get(j, ()):
                        hook()
                c.block_done.more(n)

            def summed():
                act.wait_ge(S["block_done"], c.block_done.now())

            def step(ins):
                ins.then_inc(S["act_step"], 1)
                act.wait_ge(S["act_step"], c.act_step.more())

            def rsqrt_guess():
                act.wait_ge(S["ms_ready"], c.ms_ready.more())
                step(nc.scalar.activation(rs_t[:, :], ms[:, :], ACT.Ln))
                nc.scalar.activation(rs[:, :], rs_t[:, :], ACT.Exp, scale=-0.5).then_inc(S["rs_guess"], 1)

            def square_sum(src, o, junk):
                if c.sumsq_ready.n:
                    act.wait_ge(S["sumsq_ready"], c.sumsq_ready.now())
                c.sumsq_ready.more()
                nc.scalar.activation(junk, src, ACT.Square, accum_out=o).then_inc(S["sumsq_ready"], 1)

            for t in range(NT):
                act.dma_start(x_tok[:, t, :], x[t]).then_inc(S[f"x_landed{t}"], 16)
            act.dma_start(ws_raw[:, :, :], wsmall).then_inc(S["small_landed"], 16)
            act.dma_start(par[:, :], params).then_inc(S["small_landed"], 16)
            act.dma_start(w_gate_sb[:, :], w_gate).then_inc(S["small_landed"], 16)
            act.dma_start(w2_sb[:, :, :, :], w2).then_inc(S["small_landed"], 16)
            act.dma_start(g_gla_bc[:, :], g_gla.broadcast_to([P, HV])).then_inc(S["small_landed"], 16)

            for t in range(NT):
                act.wait_ge(S[f"x_landed{t}"], 16)
                square_sum(x_tok[:, t, :], sumsq[:, t, 0:1], square_junk[:, :])
            rsqrt_guess()
            act.wait_ge(S["small_landed"], 80)
            nc.scalar.activation(ws_hi[:, :, :], ws_raw[:, :, :], ACT.Copy).then_inc(S["ws_hi_ready"], 1)
            for _ in range(LEAD):
                split()
            for f in range(KT // 4):
                for b in range(2):
                    act.wait_ge(S[f"tp_ready{b}"], c[f"tp_ready{b}"].more())
                    for kk in range(2):
                        k = 4 * f + 2 * b + kk
                        nc.scalar.activation(h_hi[:, k, :], tp[b][:, kk * SEQ:(kk + 1) * SEQ], ACT.Copy,
                                             scale=par[:, C_GMIX + k:C_GMIX + k + 1]).then_inc(S["tp_hi"], 1)
            c.tp_hi.more(KT)
            act.wait_ge(S["small_ready"], 1)
            nc.scalar.activation(z_small[:, :, :], mix[0][:, 0:NT * NSMALL].rearrange("p (t n) -> p t n", t=NT),
                                 ACT.Copy).then_inc(S["z_small_ready"], 1)
            act.wait_ge(S["z_small_ready"], 1)
            nc.scalar.activation(branch_gate[:, :, :, :].rearrange("p t n h -> p t (n h)"),
                                 z_small[:, :, GATE_RANK:NSMALL], ACT.Exp, scale=-1.0).then_inc(S["branch_e"], 1)

            def stage_tile():
                summed()
                for b in range(2):
                    act.wait_ge(S[f"tp_ready{b}"], c[f"tp_ready{b}"].now())
                nc.scalar.activation(staging[:, 0, :], acc[0][0][:, :], ACT.Copy).then_inc(S["staging_full"], 1)
                c.staging_full.more(2)

            def store_T(dest):
                act.wait_ge(S["tp_ready0"], c.tp_ready0.more())
                c.tp_ready1.more()
                nc.scalar.activation(dest[:, 0:2, :], tp[0][:, :].rearrange("p (f s) -> p f s", f=2),
                                     ACT.Copy).then_inc(S["tp_free0"], 1)

            def feature_major(trips, dest, hooks=lambda i: {}, **more):
                pers = dict(LOOP, tp_ready0=1, tp_ready1=1, staging_full=2)
                pers.update(more)
                with c.loop(act, trips, **pers) as i:
                    blocks(hooks=hooks(i))
                    stage_tile()
                    store_T(dest(i))

            def copy_tile(dest, pair):
                summed()
                nc.scalar.activation(dest, acc[pair][0][:, :], ACT.Copy).then_inc(S[f"acc_free{pair}"], 1)

            def flat_split(n):
                act.wait_ge(S["flat_ready"], 2 * (n + 1))
                nc.scalar.activation(flat_hi[n][:, :, :], flat[n][:, :, :, :].rearrange("p l h j -> p l (h j)"),
                                     ACT.Copy).then_inc(S["flat_hi_ready"], 1)

            feature_major(2, lambda i: kvc_T[:, i, :, :])
            act.wait_ge(S["glr_ready"], 1)
            nc.scalar.activation(glr_T[:, :], mix[1][0:GATE_RANK, 0:SEQ], ACT.Copy).then_inc(S["glr_T_ready"], 1)
            flat_split(0)
            feature_major(2, lambda i: ksw_T[:, i, :, :])
            flat_split(1)
            for n in range(2):
                blocks()
                copy_tile(vsw[:, n, 0, :], n)

            blocks()
            blocks()
            summed()
            for n in range(2):
                nc.scalar.activation(hid_e[:, n, :], acc[1][n][0:NC4, 0:CMP_HIDDEN], ACT.Exp,
                                     scale=-1.0).then_inc(S["hid_e_ready"], 1)
            act.wait_ge(S["hid_tp"], 1)
            nc.scalar.activation(hid_T[:, :, 0:NC4], mix[0][:, 0:256].rearrange("p (a n) -> p a n", a=4)[:, :, 0:NC4],
                                 ACT.Copy).then_inc(S["hid_T_ready"], 1)
            act.wait_ge(S["cmp_out"], 1)
            nc.scalar.activation(k_cmp_T[:, :], mix[1][:, 0:NC4], ACT.Copy).then_inc(S["cmp_sb"], 1)

            act.wait_ge(S["nega_ready"], 1)
            step(nc.scalar.activation(log_a[:, :], log_a[:, :], ACT.Exp))
            nc.scalar.activation(log_a[:, :], log_a[:, :], ACT.Ln, bias=1.0).then_inc(S["ln_ready"], 1)
            feature_major(2, lambda i: gqk_blocks[:, i, :, :])
            feature_major(2, lambda i: gqk_blocks[:, i + 2, :, :])
            with c.loop(act, 2, **LOOP2) as i:
                for n in range(2):
                    blocks()
                    copy_tile(gv[:, i * 2 + n, 0, :], n)
            with c.loop(act, 2, **LOOP2) as i:
                for n in range(2):
                    blocks()
                    summed()
                    for t in range(NT):
                        nc.scalar.activation(r_gate[n][:, t, :], acc[n][t][:, :], ACT.Exp,
                                             scale=-1.0).then_inc(S["gr_e"], 1)

            def gla_exps(i):
                def go():
                    nc.scalar.activation(e_pos[:, :, :, :].rearrange("p f n c -> p (f n) c"),
                                         decay_sum[:, i, :, :], ACT.Exp, scale=1.0 / TAU)
                    nc.scalar.activation(e_neg[:, :, :, :].rearrange("p f n c -> p (f n) c"),
                                         decay_sum[:, i, :, :], ACT.Exp, scale=-1.0 / TAU)
                    act.wait_ge(S["decay_ready"], c.decay_ready.more())
                    nc.scalar.activation(e_end[:, :, :, :], e_end[:, :, :, :], ACT.Exp,
                                         scale=1.0 / TAU).then_inc(S["exp_ready"], 1)
                return go

            def gla_norm():
                act.wait_ge(S["gla_o_ready"], c.gla_o_ready.more())
                for t in range(NT):
                    square_sum(acc[1][t][:, :], sumsq[:, t, 0:1], mix[1][:, :])
                rsqrt_guess()
                c.staging_full.more(2)

            def gla_store(i):
                return lambda: store_T(og_T[:, i, :, :])

            feature_major(GLA_HEADS, lambda i: nq_T[:, i, :, :],
                          lambda i: {0: [gla_exps(i)], 3: [gla_norm], 5: [gla_store(i)]},
                          tp_ready0=2, tp_ready1=2, staging_full=4, decay_ready=1, gla_o_ready=1, ms_ready=1,
                          act_step=1, sumsq_ready=2)

            def split_chunks(src, hi, done):
                for n in range(4):
                    nc.scalar.activation(hi[:, 4 * n:4 * n + 4, :], src[:, n, :, :], ACT.Copy).then_inc(S[done], 1)

            for b in range(2):
                act.wait_ge(S[f"tp_free{b}"], c[f"tp_ready{b}"].now())
            split_chunks(og_T, og_hi, "og_hi_ready")

            def cmp_exp():
                act.wait_ge(S["cs_sub"], c.cs_sub.more())
                nc.scalar.activation(p_c[:, :, :, 0:NCMP], p_c[:, :, :, 0:NCMP], ACT.Exp).then_inc(S["cs_exp"], 1)

            def exps():
                act.wait_ge(S["nmax_ready"], c.nmax_ready.more())
                for t in range(NT):
                    for n in range(2):
                        at_col, width = (n * P, P) if t == 0 else (SEQ + n * SEQ, SEQ)
                        part = p_sc[:, at_col:at_col + width]
                        end = nc.scalar.activation(part, part, ACT.Exp, bias=nmax[:, t, n:n + 1],
                                                   accum_out=coef[:, t, n:n + 1])
                end.then_inc(S["p_exp"], 1)

            def store_p():
                act.wait_ge(S["tp_ready0"], c.tp_ready0.more())
                c.tp_ready1.more()
                nc.scalar.activation(p_T[:, 0, 0:3 * P], tp[0][:, 0:3 * P], ACT.Copy)
                nc.scalar.activation(p_T[0:NCMP, 0, 3 * P:4 * P], tp[0][0:NCMP, 3 * P:4 * P],
                                     ACT.Copy).then_inc(S["tp_free0"], 1)

            def store_o(i, u):
                def go():
                    act.wait_ge(S["pv_ready"], c.pv_ready.more())
                    nc.scalar.activation(on_T[:, i, u, :], tp[0][:, 0:SEQ], ACT.Copy).then_inc(
                        S["on_ready"], 1)
                return go

            def gate_exp():
                summed()
                for t in range(NT):
                    nc.scalar.activation(gate[:, t, :], acc[0][t][:, :], ACT.Exp, scale=-1.0).then_inc(
                        S["acc_free0"], 1)

            with c.loop(act, KV_HEADS, **dict(LOOP2, tp_ready0=4, tp_ready1=4, cs_sub=1, nmax_ready=4,
                                              pv_ready=4)) as i:
                blocks(hooks={0: [cmp_exp, exps], 3: [store_p, exps], 4: [store_o(i, 0)],
                              6: [store_p, exps], 7: [store_o(i, 1)]})
                gate_exp()
                blocks(hooks={1: [store_p, exps], 2: [store_o(i, 2)], 5: [store_p], 6: [store_o(i, 3)]})

            act.wait_ge(S["on_ready"], HEADS)
            summed()
            split_chunks(on_T, on_hi, "on_hi_ready")
            for t in range(NT):
                act.dma_start(x1[:, t, :], x[t]).then_inc(S["xres_landed"], 16)

            def tp_split(hi, scales=None):
                for b in range(2):
                    act.wait_ge(S[f"tp_ready{b}"], c[f"tp_ready{b}"].more())
                    if scales is None:
                        nc.scalar.activation(hi[:, 2 * b:2 * b + 2, :], tp[b][:, :].rearrange("p (f s) -> p f s", f=2),
                                             ACT.Copy).then_inc(S["tp_hi"], 1)
                    else:
                        for f in range(2):
                            nc.scalar.activation(hi[:, 2 * b + f, :], tp[b][:, f * SEQ:(f + 1) * SEQ], ACT.Copy,
                                                 scale=scales(2 * b + f)).then_inc(S["tp_hi"], 1)

            with c.loop(act, 4, **dict(LOOP2, tp_ready0=1, tp_ready1=1, staging_full=2)) as i:
                blocks()
                gate_exp()
                blocks()
                c.staging_full.more(2)
                tp_split(blocks_of(m_hi)[:, i, :, :])


            for i in range(4):
                blocks()
                act.wait_ge(S["staging_full"], c.staging_full.more(2))
                nc.scalar.activation(x1[:, :, i * COL:(i + 1) * COL], staging[:, :, :], ACT.Copy)
                for t in range(NT):
                    square_sum(staging[:, t, :], sumsq[:, t, i:i + 1], mix[0][:, :])
                tp_split(blocks_of(f_hi)[:, i, :, :], lambda f: par[:, C_GFFN + 4 * i + f:C_GFFN + 4 * i + f + 1])
            act.dma_start(g_fin_bc[:, :], g_final.broadcast_to([P, D])).then_inc(S["gfin_landed"], 16)
            rsqrt_guess()

            act.wait_ge(S["rs_ready"], 1)
            with c.loop(act, FFB, **dict(LOOP2, tp_ready0=1, tp_ready1=1)) as i:
                blocks()
                summed()
                for t in range(NT):
                    nc.scalar.activation(ffn_gate[:, t, :], acc[0][t][:, :], ACT.Sigmoid,
                                         scale=rs[:, t:t + 1]).then_inc(S["gate_e"], 1)
                blocks()
                tp_split(act_hi[:, :, :].rearrange("p (a f) s -> p a f s", f=4)[:, i, :, :])
            c.acc_free0.more(2 * (5 + 4 + 4 + FFB))
            c.acc_free1.more(2 * (5 + 4 + 4))
            for n in range(4):
                blocks(NDOWN, splits=NDOWN if n < 3 else NDOWN - LEAD)
                for t in range(NT):
                    added = c[f"acc_free{n % 2}"]
                    act.wait_ge(added.sem, added.more())
                    square_sum(x1[:, t, n * COL:(n + 1) * COL], sumsq[:, t, n:n + 1], mix[0][:, :])
            rsqrt_guess()

        @block.vector
        def _(dve):
            c = Counts(S)
            LOOP = dict(lo_ready=NCOL, block_done=NCOL)
            LOOP2 = {n: 2 * v for n, v in LOOP.items()}

            def split():
                s = c.lo_ready.n % SLOTS
                dve.wait_ge(S["hi_ready"], c.lo_ready.more())
                nc.vector.tensor_tensor(w_lo[s][:, :], w_raw[s][:, :], f32(w_hi[s][:, :]),
                                        ALU.subtract).then_inc(S["lo_ready"], 1)

            def blocks(n=NCOL, hooks={}, splits=None):
                for j in range(n):
                    if splits is None or j < splits:
                        split()
                    for hook in hooks.get(j, ()):
                        hook()
                c.block_done.more(n)

            def summed():
                dve.wait_ge(S["block_done"], c.block_done.now())

            def step(ins):
                ins.then_inc(S["dve_step"], 1)
                dve.wait_ge(S["dve_step"], c.dve_step.more())

            def mean_squares(src, n):
                nc.vector.tensor_scalar(ms[:, :], src, 1.0 / n, EPS, ALU.mult, ALU.add).then_inc(S["ms_ready"], 1)

            def rsqrt_refine():
                dve.wait_ge(S["rs_guess"], c.rs_guess.more())
                step(nc.vector.tensor_tensor(rs_t[:, :], rs[:, :], rs[:, :], ALU.mult))
                step(nc.vector.tensor_tensor(rs_t[:, :], rs_t[:, :], ms[:, :], ALU.mult))
                step(nc.vector.tensor_scalar(rs_t[:, :], rs_t[:, :], -0.5, 1.5, ALU.mult, ALU.add))
                step(nc.vector.tensor_tensor(rs[:, :], rs[:, :], rs_t[:, :], ALU.mult))

            def sum_waits(n=NT):
                dve.wait_ge(S["sumsq_ready"], c.sumsq_ready.more(n))

            sum_waits()
            mean_squares(sumsq[:, :, 0], D)
            rsqrt_refine()
            for t in range(NT):
                nc.vector.tensor_scalar(x_tok[:, t, :], x_tok[:, t, :], rs[:, t:t + 1], None,
                                        ALU.mult).then_inc(S["h_tok_ready"], 1)
            dve.wait_ge(S["ws_hi_ready"], 1)
            nc.vector.tensor_tensor(ws_lo[:, :, :], ws_raw[:, :, :], f32(ws_hi[:, :, :]),
                                    ALU.subtract).then_inc(S["ws_lo_ready"], 1)
            for _ in range(LEAD):
                split()
            for f in range(KT // 4):
                for b in range(2):
                    c[f"tp_ready{b}"].more()
                    dve.wait_ge(S["tp_hi"], c.tp_hi.more(2))
                    for kk in range(2):
                        k = 4 * f + 2 * b + kk
                        end = nc.vector.scalar_tensor_tensor(
                            h_lo[:, k, :], tp[b][:, kk * SEQ:(kk + 1) * SEQ], par[:, C_GMIX + k:C_GMIX + k + 1],
                            f32(h_hi[:, k, :]), ALU.mult, ALU.subtract)
                    end.then_inc(S[f"tp_free{b}"], 1)
            dve.wait_ge(S["branch_e"], 1)
            step(nc.vector.tensor_scalar(branch_gate[:, :, :, :], branch_gate[:, :, :, :], 1.0, None, ALU.add))
            step(nc.vector.reciprocal(branch_gate[:, :, :, :], branch_gate[:, :, :, :]))

            def staging_free():
                for b in range(2):
                    dve.wait_ge(S[f"tp_ready{b}"], c[f"tp_ready{b}"].now())

            def stage_tile():
                summed()
                staging_free()
                nc.vector.tensor_copy(staging[:, 1, :], acc[0][1][:, :]).then_inc(S["staging_full"], 1)

            def store_T(dest):
                c.tp_ready0.more()
                dve.wait_ge(S["tp_ready1"], c.tp_ready1.more())
                nc.vector.tensor_copy(dest[:, 2:4, :], tp[1][:, :].rearrange("p (f s) -> p f s", f=2)).then_inc(
                    S["tp_free1"], 1)

            def stored():
                for b in range(2):
                    dve.wait_ge(S[f"tp_free{b}"], c[f"tp_ready{b}"].now())

            def feature_major(trips, dest, hooks=lambda i: {}, **more):
                pers = dict(LOOP, tp_ready0=1, tp_ready1=1)
                pers.update(more)
                with c.loop(dve, trips, **pers) as i:
                    blocks(hooks=hooks(i))
                    stage_tile()
                    store_T(dest(i))

            def copy_tile(dest, pair):
                summed()
                nc.vector.tensor_copy(dest, acc[pair][1][:, :]).then_inc(S[f"acc_free{pair}"], 1)

            def flatten_blocks(n):
                stored()
                col = (C_PEK, C_PEV)[n]
                for half in range(2):
                    tokens = kvc_T[:, n, :, half * STRIDE:half * STRIDE + NCMP * STRIDE]
                    src = tokens.rearrange("p h (j l) -> p l h j", l=STRIDE)
                    pe_cols = par[:, col + half * STRIDE:col + (half + 1) * STRIDE]
                    pe_all = pe_cols.rearrange("p (l a b) -> p l a b", a=1, b=1).broadcast_to(
                        [P, STRIDE, KV_HEADS, NCMP])
                    nc.vector.tensor_tensor(flat[n][:, half * STRIDE:(half + 1) * STRIDE, :, :], src, pe_all,
                                            ALU.add).then_inc(S["flat_ready"], 1)
                dve.wait_ge(S["flat_hi_ready"], n + 1)
                nc.vector.tensor_tensor(flat_lo[n][:, :, :], flat[n][:, :, :, :].rearrange("p l h j -> p l (h j)"),
                                        f32(flat_hi[n][:, :, :]), ALU.subtract).then_inc(S["flat_lo_ready"], 1)

            feature_major(2, lambda i: kvc_T[:, i, :, :])
            flatten_blocks(0)
            feature_major(2, lambda i: ksw_T[:, i, :, :])
            flatten_blocks(1)
            for n in range(2):
                blocks()
                copy_tile(vsw[:, n, 1, :], n)

            blocks()
            blocks()
            dve.wait_ge(S["hid_e_ready"], 2)
            step(nc.vector.tensor_scalar(hid_e[:, :, :], hid_e[:, :, :], 1.0, None, ALU.add))
            step(nc.vector.reciprocal(hid_e[:, :, :], hid_e[:, :, :]))
            for n in range(2):
                end = nc.vector.tensor_tensor(hid[:, n, :], acc[1][n][0:NC4, 0:CMP_HIDDEN], hid_e[:, n, :], ALU.mult)
            end.then_inc(S["hid_sb_ready"], 1)
            dve.wait_ge(S["cmp_out"], 1)
            nc.vector.tensor_copy(v_cmp[:, :, :], mix[0][0:NCMP, :].rearrange("p (g d) -> p g d", g=KV_HEADS)).then_inc(
                S["cmp_sb"], 1)

            dve.wait_ge(S["gate_mm"], 1)
            gate_banks = [acc[1][0], acc[1][1], mix[0], mix[1]]
            a_all = decay_sum[:, :, :, :].rearrange("p h n c -> p (h n c)")
            for f in range(GLA_DK // P):
                nc.vector.tensor_scalar(a_all[:, f * SEQ:(f + 1) * SEQ],
                                        gate_banks[f // 2][:, (f % 2) * SEQ:(f % 2 + 1) * SEQ],
                                        par[:, C_BG + f:C_BG + f + 1], None, ALU.add).then_inc(S["gate_sb"], 1)
            dve.wait_ge(S["gate_sb"], GLA_DK // P)
            nc.vector.scalar_tensor_tensor(log_a[:, :], a_all, -1.0, a_all, ALU.mult, ALU.min).then_inc(
                S["nega_ready"], 1)
            feature_major(2, lambda i: gqk_blocks[:, i, :, :])
            dve.wait_ge(S["ln_ready"], 1)
            step(nc.vector.scalar_tensor_tensor(log_a[:, :], a_all, 0.0, log_a[:, :], ALU.min, ALU.subtract))
            feature_major(2, lambda i: gqk_blocks[:, i + 2, :, :])
            step(nc.vector.memset(chunk_keep[:, :], 1.0))
            step(nc.vector.memset(chunk_keep[:, :].rearrange("p (n c) -> p n c", c=CHUNK)[:, :, 0:1], 0.0))
            step(nc.vector.tensor_tensor_scan(a_all, chunk_keep[:, :], log_a[:, :], 0.0, ALU.mult, ALU.add))
            with c.loop(dve, 2, **LOOP2) as i:
                for n in range(2):
                    blocks()
                    copy_tile(gv[:, i * 2 + n, 1, :], n)
            with c.loop(dve, 2, **dict(LOOP2, gr_e=4, dve_step=6)) as i:
                for n in range(2):
                    blocks()
                    dve.wait_ge(S["gr_e"], c.gr_e.more(2))
                    r = r_gate[n][:, :, :]
                    step(nc.vector.tensor_scalar(r, r, 1.0, None, ALU.add))
                    step(nc.vector.reciprocal(r, r))
                    gain = g_gla_bc[:, :].rearrange("p (a n) -> p a n", a=1).broadcast_to([P, NT, HV])
                    step(nc.vector.tensor_tensor(r, r, gain, ALU.mult))
                    for t in range(NT):
                        nc.vector.tensor_tensor(gr[:, i * 2 + n, t, :], acc[n][t][:, :], r[:, t, :], ALU.mult).then_inc(S[f"acc_free{n}"], 1)

            def gla_decays(i):
                def go():
                    b = decay_sum[:, i, :, :]
                    last = decay_sum[:, i, :, CHUNK - 1:CHUNK].broadcast_to([P, FT * NCH, CHUNK])
                    nc.vector.tensor_tensor(e_end[:, :, :, :].rearrange("p f n c -> p (f n) c"), last, b,
                                            ALU.subtract).then_inc(S["decay_ready"], 1)
                return go

            def gla_ops(i):
                def go():
                    dve.wait_ge(S["exp_ready"], c.exp_ready.more())
                    flat4 = "p f n c -> p (f n c)"
                    q = gqk_T[:, 0, i, :, :].rearrange("p f s -> p (f s)")
                    k = gqk_T[:, 1, i, :, :].rearrange("p f s -> p (f s)")
                    ep, en, ee, qd = (v[:, :, :, :].rearrange(flat4) for v in (e_pos, e_neg, e_end, q_dec))
                    nc.vector.tensor_tensor(en, k, en, ALU.mult)
                    nc.vector.tensor_tensor(ee, k, ee, ALU.mult)
                    step(nc.vector.scalar_tensor_tensor(qd, q, float(HK) ** -0.5, ep, ALU.mult, ALU.mult))
                    step(nc.vector.tensor_tensor(
                        q2[:, :, :, :], q_dec[:, :, 2:4, :],
                        e_pos[:, :, 1:3, CHUNK - 1:CHUNK].broadcast_to([P, FT, 2, CHUNK]), ALU.mult))
                    nc.vector.tensor_tensor(
                        q3[:, :, :], q2[:, :, 1, :],
                        e_pos[:, :, 1, CHUNK - 1:CHUNK].broadcast_to([P, FT, CHUNK]), ALU.mult).then_inc(
                            S["gla_ops"], 1)
                return go

            def gla_mask():
                dve.wait_ge(S["gla_attn"], c.gla_attn.more())
                nc.vector.tensor_copy(attn_sb[:, 1, :], mix[0][:, P:2 * P])
                for tile in (0, 2):
                    for row in (0, CHUNK):
                        rows = slice(row, row + CHUNK)
                        end = nc.vector.copy_predicated(
                            attn_sb[rows, tile, row:P], gla_valid[rows, row:P].bitcast(I32),
                            mix[0][rows, tile * P + row:(tile + 1) * P])
                end.then_inc(S["attn_ready"], 1)

            def gla_norm(i):
                def go():
                    sum_waits()
                    mean_squares(sumsq[:, :, 0], HV)
                    rsqrt_refine()
                    staging_free()
                    for t in range(NT):
                        nc.vector.scalar_tensor_tensor(staging[:, t, :], acc[1][t][:, :], rs[:, t:t + 1],
                                                       gr[:, i, t, :], ALU.mult, ALU.mult).then_inc(
                                                           S["staging_full"], 1)
                return go

            feature_major(GLA_HEADS, lambda i: nq_T[:, i, :, :],
                          lambda i: {0: [gla_decays(i)], 1: [gla_ops(i)], 2: [gla_mask], 3: [gla_norm(i)],
                                     5: [lambda: store_T(og_T[:, i, :, :])]},
                          tp_ready0=2, tp_ready1=2, exp_ready=1, gla_attn=1, sumsq_ready=2, rs_guess=1, dve_step=6)

            def split_chunks(src, hi, lo, hi_sem, lo_sem):
                for n in range(4):
                    dve.wait_ge(S[hi_sem], n + 1)
                    nc.vector.tensor_tensor(lo[:, 4 * n:4 * n + 4, :], src[:, n, :, :],
                                            f32(hi[:, 4 * n:4 * n + 4, :]), ALU.subtract).then_inc(S[lo_sem], 1)

            split_chunks(og_T, og_hi, og_lo, "og_hi_ready", "og_lo_ready")

            def per_query(v):
                return v[:, :, 0:NCMP].rearrange("p (a t) c -> p a t c", a=1).broadcast_to([P, GROUP, NT, NCMP])

            def per_key(v):
                return v[:, :, :].rearrange("p u (t a) -> p u t a", a=1).broadcast_to([P, GROUP, NT, NCMP])

            pc = p_c[:, :, :, 0:NCMP]

            def cmp_max():
                dve.wait_ge(S["cs_ready"], c.cs_ready.more())
                cs = tp[1][:, 0:GROUP * NT * STRIDE].rearrange("p (u t c) -> p u t c", u=GROUP, t=NT)
                step(nc.vector.tensor_tensor(pc, cs[:, :, :, 0:NCMP], per_query(cmp_bias), ALU.add))
                step(nc.vector.tensor_reduce(max_c[:, :, :], pc, AX.X, ALU.max))
                nc.vector.tensor_tensor(pc, pc, per_key(max_c), ALU.subtract).then_inc(S["cs_sub"], 1)

            def cmp_weights(i):
                def go():
                    dve.wait_ge(S["cs_exp"], c.cs_exp.more())
                    step(nc.vector.tensor_reduce(coef_c[:, :, :], pc, AX.X, ALU.add))
                    step(nc.vector.reciprocal(coef_c[:, :, :], coef_c[:, :, :]))
                    gates = branch_gate[:, :, 0, bass.ds(i * GROUP, GROUP)].rearrange("p t u -> p u t")
                    step(nc.vector.tensor_tensor(coef_c[:, :, :], coef_c[:, :, :], gates, ALU.mult))
                    step(nc.vector.tensor_tensor(pc, pc, per_query(cmp_valid), ALU.mult))
                    step(nc.vector.tensor_tensor(pc, pc, per_key(coef_c), ALU.mult))
                return go

            early = p_sc[:, 0:SEQ].rearrange("p (n s) -> p n s", n=2)
            late = p_sc[:, SEQ:3 * SEQ].rearrange("p (n s) -> p n s", n=2)

            def maxima():
                dve.wait_ge(S["qk_ready"], c.qk_ready.more())
                tri = causal_bias[:, P:SEQ].rearrange("p (a s) -> p a s", a=1).broadcast_to([P, 2, P])
                both = causal_bias[:, :].rearrange("p (a s) -> p a s", a=1).broadcast_to([P, 2, SEQ])
                nc.vector.tensor_tensor(early, mix[0][:, 0:SEQ].rearrange("p (n s) -> p n s", n=2), tri, ALU.add)
                step(nc.vector.tensor_tensor(late, mix[1][:, :].rearrange("p (n s) -> p n s", n=2), both, ALU.add))
                nc.vector.tensor_reduce(nmax[:, 0, :], early, AX.X, ALU.max, negate=True)
                nc.vector.tensor_reduce(nmax[:, 1, :], late, AX.X, ALU.max, negate=True).then_inc(
                    S["nmax_ready"], 1)

            def weights(i, u):
                def go():
                    dve.wait_ge(S["p_exp"], c.p_exp.more())
                    step(nc.vector.reciprocal(coef[:, :, :], coef[:, :, :]))
                    gates = branch_gate[:, :, 1:3, bass.ds(i * GROUP + u, 1)].rearrange("p t n a -> p t (n a)")
                    step(nc.vector.tensor_tensor(coef[:, :, :], coef[:, :, :], gates, ALU.mult))
                    for t, part, width in ((0, early, P), (1, late, SEQ)):
                        by = coef[:, t, :].rearrange("p (n a) -> p n a", a=1).broadcast_to([P, 2, width])
                        end = nc.vector.tensor_tensor(part, part, by, ALU.mult)
                    end.then_inc(S["p_ready"], 1)
                return go

            def store_p():
                c.tp_ready0.more()
                dve.wait_ge(S["tp_ready1"], c.tp_ready1.more())
                nc.vector.tensor_copy(p_T[:, 1, 0:3 * P], tp[1][:, 0:3 * P])
                nc.vector.tensor_copy(p_T[0:NCMP, 1, 3 * P:4 * P], tp[1][0:NCMP, 3 * P:4 * P]).then_inc(
                    S["tp_free1"], 1)

            def merge_gate():
                dve.wait_ge(S["acc_free0"], c.acc_free0.more(2))
                step(nc.vector.tensor_scalar(gate[:, :, :], gate[:, :, :], 1.0, None, ALU.add))
                step(nc.vector.reciprocal(gate[:, :, :], gate[:, :, :]))

            c.acc_free0.more(2 * 5)
            stored()
            with c.loop(dve, KV_HEADS, **dict(LOOP2, tp_ready0=4, tp_ready1=4, cs_ready=1, cs_exp=1, qk_ready=4,
                                              p_exp=4, acc_free0=2, dve_step=2 + 5 + 4 + 8 + 2)) as i:
                nc.vector.tensor_scalar(q_st[:, :, :], nq_T[:, i, :, :], float(HD) ** -0.5, None,
                                        ALU.mult).then_inc(S["q_st_ready"], 1)
                nc.vector.tensor_copy(v_st[:, :, :, :].rearrange("p n t d -> p (n t) d"),
                                      vsw[:, :, :, bass.ds(i * HD, HD)].rearrange("p n t d -> p (n t) d"))
                nc.vector.tensor_copy(vc_st[:, :], v_cmp[:, i, :]).then_inc(S["v_st_ready"], 1)
                blocks(hooks={0: [cmp_max, maxima], 1: [cmp_weights(i), weights(i, 0)], 3: [store_p, maxima],
                              4: [weights(i, 1)], 6: [store_p, maxima], 7: [weights(i, 2)]})
                merge_gate()
                blocks(hooks={1: [store_p, maxima], 2: [weights(i, 3)], 5: [store_p]})
                summed()
                for t in range(NT):
                    nc.vector.tensor_tensor(merged[:, i, t, :], acc[1][t][:, :], gate[:, t, :],
                                            ALU.mult).then_inc(S["acc_free1"], 1)
            split_chunks(on_T, on_hi, on_lo, "on_hi_ready", "on_lo_ready")

            def tp_split(hi, lo, scales=None):
                for b in range(2):
                    c[f"tp_ready{b}"].more()
                    if scales is None:
                        dve.wait_ge(S["tp_hi"], c.tp_hi.more())
                        end = nc.vector.tensor_tensor(lo[:, 2 * b:2 * b + 2, :],
                                                      tp[b][:, :].rearrange("p (f s) -> p f s", f=2),
                                                      f32(hi[:, 2 * b:2 * b + 2, :]), ALU.subtract)
                    else:
                        dve.wait_ge(S["tp_hi"], c.tp_hi.more(2))
                        for f in range(2):
                            end = nc.vector.scalar_tensor_tensor(
                                lo[:, 2 * b + f, :], tp[b][:, f * SEQ:(f + 1) * SEQ], scales(2 * b + f),
                                f32(hi[:, 2 * b + f, :]), ALU.mult, ALU.subtract)
                    end.then_inc(S[f"tp_free{b}"], 1)

            c.acc_free1.more(2 * 9)
            with c.loop(dve, 4, **dict(LOOP2, tp_ready0=1, tp_ready1=1, tp_hi=2, acc_free0=2, acc_free1=2,
                                       dve_step=2)) as i:
                blocks()
                merge_gate()
                blocks()
                summed()
                for t in range(NT):
                    nc.vector.tensor_tensor(gate[:, t, :], acc[1][t][:, :], gate[:, t, :],
                                            ALU.mult).then_inc(S["acc_free1"], 1)
                dve.wait_ge(S["acc_free1"], c.acc_free1.more(2))
                staging_free()
                for t in range(NT):
                    nc.vector.tensor_tensor(staging[:, t, :], gate[:, t, :], merged[:, i, t, :],
                                            ALU.add).then_inc(S["staging_full"], 1)
                tp_split(blocks_of(m_hi)[:, i, :, :], blocks_of(m_lo)[:, i, :, :])

            dve.wait_ge(S["xres_landed"], 16 * NT)
            with c.loop(dve, 4, **dict(LOOP, tp_ready0=1, tp_ready1=1, tp_hi=4)) as i:
                blocks()
                summed()
                staging_free()
                for t in range(NT):
                    nc.vector.tensor_tensor(staging[:, t, :], acc[0][t][:, :], x1[:, t, bass.ds(i * COL, COL)],
                                            ALU.add).then_inc(S["staging_full"], 1)
                tp_split(blocks_of(f_hi)[:, i, :, :], blocks_of(f_lo)[:, i, :, :],
                         lambda f: par[:, bass.ds(i * 4 + (C_GFFN + f), 1)])

            def row_norms():
                sum_waits(4 * NT)
                step(nc.vector.tensor_reduce(rs_t[:, :], sumsq[:, :, :], AX.X, ALU.add))
                mean_squares(rs_t[:, :], D)
                rsqrt_refine()

            row_norms()
            nc.vector.tensor_copy(rs_t[:, :], rs[:, :]).then_inc(S["rs_ready"], 1)

            with c.loop(dve, FFB, **dict(LOOP2, tp_ready0=1, tp_ready1=1, tp_hi=2, gate_e=2)) as i:
                blocks()
                dve.wait_ge(S["gate_e"], c.gate_e.more(2))
                for t in range(NT):
                    nc.vector.scalar_tensor_tensor(ffn_gate[:, t, :], acc[0][t][:, :], rs[:, t:t + 1],
                                                   ffn_gate[:, t, :], ALU.mult, ALU.mult).then_inc(S["acc_free0"], 1)
                blocks()
                summed()
                staging_free()
                for t in range(NT):
                    nc.vector.scalar_tensor_tensor(staging[:, t, :], acc[1][t][:, :], rs[:, t:t + 1],
                                                   ffn_gate[:, t, :], ALU.mult, ALU.mult).then_inc(
                                                       S["staging_full"], 1)
                tp_split(act_hi[:, :, :].rearrange("p (a f) s -> p a f s", f=4)[:, i, :, :],
                         act_lo[:, :, :].rearrange("p (a f) s -> p a f s", f=4)[:, i, :, :])
            for n in range(4):
                blocks(NDOWN, splits=NDOWN if n < 3 else NDOWN - LEAD)
                summed()
                for t in range(NT):
                    part = x1[:, t, n * COL:(n + 1) * COL]
                    nc.vector.tensor_tensor(part, acc[n % 2][t][:, :], part, ALU.add).then_inc(
                        S[f"acc_free{n % 2}"], 1)
            row_norms()
            dve.wait_ge(S["gfin_landed"], 16)
            for t in range(NT):
                nc.vector.scalar_tensor_tensor(x1[:, t, :], x1[:, t, :], rs[:, t:t + 1], g_fin_bc[:, :],
                                               ALU.mult, ALU.mult).then_inc(S["y_ready"], 1)


def stream_blocks(w, k_tiles, cols):
    k, n = w.shape
    v = w.reshape(k // (k_tiles * P), k_tiles, P, n // cols, cols)
    return v.transpose(3, 0, 2, 1, 4).reshape(-1, P, k_tiles * cols)


def kernel(x, g_mix, w_in, w_gla_gate, b_gla_gate, g_gla_out, pe_cmp_k, w_cmp_k1, w_cmp_k2, pe_cmp_v, w_cmp_v1,
           w_cmp_v2, w_proj_gla, w_proj_nsa, w_out, g_ffn, w_ffn_gate, w_ffn_up, w_ffn_down, g_final):
    import concourse.bacc as bacc
    from concourse.bass_utils import run_bass_kernel_spmd

    def column_blocks(w):
        return stream_blocks(w, KSB, COL).reshape(w.shape[1] // COL, -1, P, SB)

    w_in = np.asarray(w_in)[0]
    kv = column_blocks(w_in[:, O_KV:O_NG])
    gates = column_blocks(w_in[:, O_MG:])
    p_gla, p_nsa = column_blocks(np.asarray(w_proj_gla)[0]), column_blocks(np.asarray(w_proj_nsa)[0])
    f_gate, f_up = column_blocks(np.asarray(w_ffn_gate)[0]), column_blocks(np.asarray(w_ffn_up)[0])
    parts = [kv[0], kv[1], kv[2], kv[4], kv[3], kv[5],
             stream_blocks(np.asarray(w_cmp_k1)[0], 4, CMP_HIDDEN), stream_blocks(np.asarray(w_cmp_v1)[0], 4, CMP_HIDDEN),
             *column_blocks(w_in[:, O_GQ:O_LR]), *column_blocks(w_in[:, O_NQ:O_KV])]
    for i in range(4):
        parts += [gates[i], p_gla[i]]
    for i in range(4):
        parts += [gates[4 + i], p_nsa[i]]
    parts += [*column_blocks(np.asarray(w_out)[0])]
    for i in range(FFB):
        parts += [f_gate[i], f_up[i]]
    parts += [*column_blocks(np.asarray(w_ffn_down)[0])]
    stream = np.concatenate(parts)
    assert stream.shape[0] == STREAM

    def by_feature(v):
        return np.asarray(v).reshape(-1, P).T

    params = np.concatenate([by_feature(g_mix), by_feature(g_ffn), by_feature(b_gla_gate),
                             np.asarray(pe_cmp_k)[0].T, np.asarray(pe_cmp_v)[0].T], axis=1)
    small = np.concatenate([w_in[:, O_LR:O_NQ], w_in[:, O_NG:O_MG]], axis=1)
    w2 = np.stack([np.asarray(w)[0].reshape(2, P, HD) for w in (w_cmp_k2, w_cmp_v2)])
    arrays = {
        "wstream": stream,
        "x": np.asarray(x).reshape(NT, P, D),
        "params": params,
        "wsmall": small.reshape(KT, P, NSMALL).transpose(1, 0, 2),
        "w_gate": np.asarray(w_gla_gate)[0],
        "w2": w2.transpose(2, 0, 1, 3),
        "g_gla": np.asarray(g_gla_out).reshape(1, HV),
        "g_final": np.asarray(g_final).reshape(1, D),
    }
    arrays = {n: np.ascontiguousarray(a) for n, a in arrays.items()}
    nc = bacc.Bacc("TRN2", target_bir_lowering=False, num_devices=1)
    args = [nc.dram_tensor(n, a.shape, F32, kind="ExternalInput").ap() for n, a in arrays.items()]
    out = nc.dram_tensor("out", (NT, P, D), F32, kind="ExternalOutput").ap()
    build(nc, *args, out)
    r = run_bass_kernel_spmd(nc, [arrays], core_ids=[0])
    return r.results[0]["out"].reshape(1, SEQ, D)
```

```python
from contextlib import ExitStack, contextmanager

import numpy as np

import concourse.bass as bass
from concourse import mybir

F32 = mybir.dt.float32
F32R = mybir.dt.float32r
I32 = mybir.dt.int32
ALU = mybir.AluOpType
ACT = mybir.ActivationFunctionType
AX = mybir.AxisListType

P = 128
SEQ = 256
NT = SEQ // P
D = 2048
KT = D // P
COL = 512
D_FF = 5632
KT_FF = D_FF // P

GLA_HEADS, GLA_DK, GLA_DV, GATE_RANK, CHUNK, TAU = 4, 1024, 2048, 16, 64, 16.0
HK, HV = GLA_DK // GLA_HEADS, GLA_DV // GLA_HEADS
FT = HK // P
NCH = SEQ // CHUNK
HEADS, KV_HEADS, HD = 16, 4, 128
GROUP = HEADS // KV_HEADS
STRIDE, CMP_LEN, CMP_HIDDEN = 16, 32, 256
NCMP = SEQ // STRIDE - 1
NC4 = KV_HEADS * NCMP
EPS = 1e-6
NEG = -1e30

O_GQ = 0
O_GK = O_GQ + GLA_DK
O_GV = O_GK + GLA_DK
O_GR = O_GV + GLA_DV
O_LR = O_GR + GLA_DV
O_NQ = O_LR + GATE_RANK
O_KV = O_NQ + HEADS * HD
O_NG = O_KV + 6 * KV_HEADS * HD
O_MG = O_NG + 3 * HEADS
IN_WIDTH = O_MG + 2 * D
NSMALL = GATE_RANK + 3 * HEADS

SB = 1024
KSB = SB // COL
SLOTS = 4
LEAD = 3
NCOL = KT // KSB
NDOWN = KT_FF // KSB
NCB = 8
FFB = D_FF // COL
STREAM = 30 * NCOL + 2 * NCB + 3 * 4 * NCOL + 2 * FFB * NCOL + 4 * NDOWN

C_GMIX, C_GFFN, C_BG, C_PEK, C_PEV = 0, KT, 2 * KT, 2 * KT + GLA_DK // P, 2 * KT + GLA_DK // P + CMP_LEN
NPAR = C_PEV + CMP_LEN


class Tally:

    def __init__(self, sem):
        self.sem, self.n, self.i, self.per = sem, 0, None, 0

    def more(self, k=1):
        self.n += k
        return self.now()

    def now(self, back=0):
        if self.i is None or self.per == 0:
            return self.n - back
        assert self.n > back, "a wait is for a value above zero"
        return self.i * self.per + (self.n - back)


class Counts:

    def __init__(self, sems):
        self.all = {n: Tally(s) for n, s in sems.items()}

    def __getattr__(self, name):
        return self.all[name]

    def __getitem__(self, name):
        return self.all[name]

    @contextmanager
    def loop(self, eng, trips, **pers):
        before = {n: t.n for n, t in self.all.items()}
        with eng.Fori(0, trips) as i:
            for n, t in self.all.items():
                t.i, t.per = i, pers.get(n, 0)
            yield i
        for n, t in self.all.items():
            assert t.n - before[n] == t.per, (n, t.n - before[n], t.per)
            t.n = before[n] + t.per * trips
            t.i, t.per = None, 0


def build(nc, wstream, x, params, wsmall, w_gate, w2, g_gla, g_final, out):
    with ExitStack() as ctx:
        base = [16512]

        def at(name, shape, dt, offset):
            return nc.alloc_sbuf_tensor_at(name, list(shape), dt, offset=offset)

        def region(size):
            r = base[0]
            base[0] += -(-size // 32) * 32
            return r

        def sb(name, shape, dt=F32):
            return at(name, shape, dt, region(4 * int(np.prod(shape[1:]))))

        K = 1024
        ident = sb("ident", [P, P])
        causal_bias = sb("causal_bias", [P, SEQ])
        gla_valid = sb("gla_valid", [P, P])
        cmp_bias = sb("cmp_bias", [P, NT, STRIDE])
        cmp_valid = sb("cmp_valid", [P, NT, STRIDE])
        par = sb("par", [P, NPAR])
        staging = sb("staging", [P, NT, COL])
        z_small = sb("z_small", [P, NT, NSMALL])
        branch_gate = sb("branch_gate", [P, NT, 3, HEADS])
        k_cmp_T = sb("k_cmp_T", [P, NC4])
        v_cmp = sb("v_cmp", [NCMP, KV_HEADS, HD])
        sumsq = sb("sumsq", [P, NT, 4])
        ms = sb("ms", [P, NT])
        rs = sb("rs", [P, NT])
        rs_h = sb("rs_h", [P, NT])
        rs_t = sb("rs_t", [P, NT])
        max_c = sb("max_c", [P, GROUP, NT])
        coef_c = sb("coef_c", [P, GROUP, NT])
        nmax = sb("nmax", [P, NT, 2])
        coef = sb("coef", [P, NT, 2])
        RS = region(5 * K)
        attn_sb = at("attn_sb", [P, 3, P], F32, RS)
        g_gla_bc = at("g_gla_bc", [P, HV], F32, RS + 1536)
        q2 = at("q2", [P, FT, 2, CHUNK], F32, RS + 3584)
        q3 = at("q3", [P, FT, CHUNK], F32, RS + 4608)
        ffn_gate = at("ffn_gate", [P, NT, COL], F32, RS)

        w_raw = [sb(f"w_raw{s}", [P, SB]) for s in range(SLOTS)]
        w_hi = [sb(f"w_hi{s}", [P, SB], F32R) for s in range(SLOTS)]
        w_lo = [sb(f"w_lo{s}", [P, SB], F32R) for s in range(SLOTS)]
        RA, RB, RG, RV, RR, RN, RX = (region(s * K) for s in (32, 16, 32, 16, 16, 16, 16))
        assert base[0] <= nc.sbuf_usable_end, (base[0], nc.sbuf_usable_end)

        h_hi = at("h_hi", [P, KT, SEQ], F32R, RA)
        h_lo = at("h_lo", [P, KT, SEQ], F32R, RA + 16 * K)
        f_hi = at("f_hi", [P, KT, SEQ], F32R, RA)
        f_lo = at("f_lo", [P, KT, SEQ], F32R, RA + 16 * K)
        x_tok = at("x_tok", [P, NT, D], F32, RV)
        square_junk = at("square_junk", [P, D], F32, RG + 16 * K)
        ws_raw = at("ws_raw", [P, KT, NSMALL], F32, RX)
        ws_hi = at("ws_hi", [P, KT, NSMALL], F32R, RX + 4 * K)
        ws_lo = at("ws_lo", [P, KT, NSMALL], F32R, RX + 8 * K)
        w2_sb = at("w2_sb", [P, 2, 2, HD], F32, RN)
        w_gate_sb = at("w_gate_sb", [GATE_RANK, GLA_DK], F32, RN + 2 * K)
        hid = at("hid", [NC4, 2, CMP_HIDDEN], F32, RN + 6 * K)
        hid_gate = at("hid_gate", [NC4, 2, CMP_HIDDEN], F32, RN + 8 * K)
        hid_T = at("hid_T", [P, 4, 64], F32, RN + 10 * K)
        glr_T = at("glr_T", [GATE_RANK, SEQ], F32, RN + 12 * K)
        ksw_T = at("ksw_T", [P, 2, KV_HEADS, SEQ], F32, RX)
        vsw = at("vsw", [P, 2, NT, COL], F32, RX + 8 * K)
        nq_T = at("nq_T", [P, KV_HEADS, GROUP, SEQ], F32, RN)
        on_T = at("on_T", [P, KV_HEADS, GROUP, SEQ], F32, RN)
        kvc_T = at("kvc_T", [P, 2, KV_HEADS, SEQ], F32, RG)
        flat_at = (RG + 8 * K, RV)
        flat = [at(f"flat{n}", [P, CMP_LEN, KV_HEADS, NCMP], F32, r) for n, r in enumerate(flat_at)]
        flat_hi = [at(f"flat_hi{n}", [P, CMP_LEN, NC4], F32R, r + 7680) for n, r in enumerate(flat_at)]
        flat_lo = [at(f"flat_lo{n}", [P, CMP_LEN, NC4], F32R, r + 15360) for n, r in enumerate(flat_at)]
        gqk_T = at("gqk_T", [P, 2, GLA_HEADS, FT, SEQ], F32, RG)
        decay_sum = at("decay_sum", [P, GLA_HEADS, FT * NCH, CHUNK], F32, RG + 16 * K)
        log_a = at("log_a", [P, GLA_HEADS * FT * SEQ], F32, RV)
        chunk_keep = at("chunk_keep", [P, GLA_HEADS * FT * SEQ], F32, RR)
        e_pos = at("e_pos", [P, FT, NCH, CHUNK], F32, RG + 24 * K)
        e_neg = at("e_neg", [P, FT, NCH, CHUNK], F32, RG + 26 * K)
        e_end = at("e_end", [P, FT, NCH, CHUNK], F32, RG + 28 * K)
        q_dec = at("q_dec", [P, FT, NCH, CHUNK], F32, RG + 30 * K)
        gv = at("gv", [P, GLA_HEADS, NT, COL], F32, RV)
        gr = at("gr", [P, GLA_HEADS, NT, COL], F32, RR)
        r_gate = [at(f"r_gate{n}", [P, NT, COL], F32, RB + 4 * K * n) for n in range(2)]
        og_hi = at("og_hi", [P, KT, SEQ], F32R, RV)
        og_lo = at("og_lo", [P, KT, SEQ], F32R, RB)
        merged = at("merged", [P, 4, NT, COL], F32, RR)
        q_st = at("q_st", [P, GROUP, SEQ], F32, RG)
        v_st = at("v_st", [P, 2, NT, HD], F32, RG + 4 * K)
        vc_st = at("vc_st", [NCMP, HD], F32, RG + 6 * K)
        p_T = at("p_T", [P, 2, COL], F32, RG + 7 * K)
        p_sc = at("p_sc", [P, 3 * SEQ], F32, RG + 11 * K)
        p_c = at("p_c", [P, GROUP, NT, STRIDE], F32, RG + 14 * K)
        gate = at("gate", [P, NT, COL], F32, RG + 16 * K)
        on_hi = at("on_hi", [P, KT, SEQ], F32R, RV)
        on_lo = at("on_lo", [P, KT, SEQ], F32R, RB)
        m_hi = at("m_hi", [P, KT, SEQ], F32R, RG)
        m_lo = at("m_lo", [P, KT, SEQ], F32R, RN)
        x1 = at("x1", [P, NT, D], F32, RX)
        act_hi = at("act_hi", [P, KT_FF, SEQ], F32R, RB)
        act_lo = at("act_lo", [P, KT_FF, SEQ], F32R, RB + 44 * K)
        g_fin_bc = at("g_fin_bc", [P, D], F32, RB + 88 * K)

        banks = [ctx.enter_context(nc.psum_tensor(f"bank{n}", [P, COL], F32)) for n in range(8)]
        acc = [banks[0:2], banks[2:4]]
        tp = banks[4:6]
        mix = banks[6:8]

        names = """x_landed0 x_landed1 x_landed2 x_landed3 par_landed small_landed xres_landed gfin_landed out_stored
            raw_landed0 raw_landed1 raw_landed2 raw_landed3 hi_ready lo_ready block_done
            acc_free0 acc_free1 tp_ready0 tp_ready1 tp_free0 tp_free1 tp_hi staging_full
            const_step const_ready keep_ready dve_step act_step sumsq_ready ms_ready root_ready rs_ready
            ws_hi_ready ws_lo_ready small_ready z_small_ready branch_gate_ready glr_ready glr_T_ready
            flat_ready flat_hi_ready flat_lo_ready hid_gate_ready hid_sb_ready hid_tp hid_T_ready cmp_out cmp_sb
            gate_mm gate_sb nega_ready ln_ready gr_gate decay_ready exp_ready gla_ops gla_attn attn_ready gla_o_ready
            q_st_ready v_st_ready cs_ready cs_sub cs_exp qk_ready nmax_ready
            p_exp p_ready pv_ready on_ready on_hi_ready on_lo_ready gate_ready y_ready""".split()
        S = {n: ctx.enter_context(nc.semaphore(n)) for n in names}
        block = ctx.enter_context(nc.Block())

        def f32(ap):
            return ap.bitcast(F32)

        def blocks_of(t):
            return t[:, :, :].rearrange("p (a f) s -> p a f s", f=4)

        gqk_blocks = gqk_T[:, :, :, :, :].rearrange("p n (a b) f s -> p (n a) (b f) s", b=2)

        @block.sync
        def _(sp):
            def load_x(s):
                sp.dma_start(x_tok[:, :, s * COL:(s + 1) * COL],
                             x[:, :, s * COL:(s + 1) * COL].rearrange("t p d -> p t d")).then_inc(
                                 S[f"x_landed{s}"], 16)

            load_x(0)
            load_x(1)
            for s in range(SLOTS):
                sp.dma_start(w_raw[s][:, :], wstream[s]).then_inc(S[f"raw_landed{s}"], 16)
                if s in (1, 2):
                    load_x(s + 1)
            with sp.Fori(1, STREAM // SLOTS) as i:
                for s in range(SLOTS):
                    sp.wait_ge(S["lo_ready"], i * SLOTS + (s - SLOTS + 1))
                    sp.dma_start(w_raw[s][:, :], wstream[i * SLOTS + s]).then_inc(S[f"raw_landed{s}"], 16)
            for n in range(2 * NT):
                t, half = n // 2, slice(n % 2 * D // 2, (n % 2 + 1) * D // 2)
                sp.wait_ge(S["y_ready"], n + 1)
                sp.dma_start(out[t][:, half], x1[:, t, half]).then_inc(S["out_stored"], 16)
            sp.wait_ge(S["out_stored"], 16 * 2 * NT)

        @block.gpsimd
        def _(pool):
            for m, v in ((ident[:, :], 0.0), (causal_bias[:, :], 0.0), (gla_valid[:, :], 1.0),
                         (cmp_bias[:, :, :], 0.0), (cmp_valid[:, :, :], 1.0), (attn_sb[:, :, :], 0.0)):
                nc.gpsimd.memset(m, v).then_inc(S["const_step"], 1)
            pool.wait_ge(S["const_step"], 6)
            diagonal = causal_bias[:, P:SEQ]
            for m, op, fill, start, pattern, per_row in (
                    (ident[:, :], ALU.not_equal, 1.0, 0, [[-1, P]], 1),
                    (diagonal, ALU.is_ge, NEG, 0, [[-1, P]], 1),
                    (gla_valid[:, :], ALU.is_ge, 0.0, 0, [[1, P]], -1),
                    (cmp_bias[:, :, :], ALU.is_ge, NEG, 1 - CMP_LEN, [[P, NT], [-STRIDE, STRIDE]], 1),
                    (cmp_valid[:, :, :], ALU.is_ge, 0.0, 1 - CMP_LEN, [[P, NT], [-STRIDE, STRIDE]], 1)):
                nc.gpsimd.affine_select(out=m, in_=m, compare_op=op, fill=fill, base=start, pattern=pattern,
                                        channel_multiplier=per_row).then_inc(S["const_ready"], 1)
            pool.wait_ge(S["hid_gate_ready"], 2)
            nc.gpsimd.memset(chunk_keep[:, :], 1.0).then_inc(S["const_step"], 1)
            pool.wait_ge(S["const_step"], 7)
            nc.gpsimd.memset(chunk_keep[:, :].rearrange("p (n c) -> p n c", c=CHUNK)[:, :, 0:1], 0.0).then_inc(
                S["keep_ready"], 1)

        @block.tensor
        def _(pe):
            c = Counts(S)

            def block_products(j, kts, width, hi, lo, outs, rows, last):
                s = c.lo_ready.n % SLOTS
                pe.wait_ge(S["lo_ready"], c.lo_ready.more())
                for kk in range(kts):
                    k = j * kts + kk
                    wh = w_hi[s][:, kk * width:(kk + 1) * width]
                    wl = w_lo[s][:, kk * width:(kk + 1) * width]
                    for t in range(len(outs)):
                        rows_t = slice(t * P, t * P + rows)
                        nc.tensor.matmul(outs[t], hi[:, k, rows_t], wh, start=k == 0, stop=False)
                        nc.tensor.matmul(outs[t], hi[:, k, rows_t], wl, start=False, stop=False)
                        end = nc.tensor.matmul(outs[t], lo[:, k, rows_t], wh, start=False, stop=k == last)
                end.then_inc(S["block_done"], 1)

            def column(pair, hi, lo, first=0, end=NCOL, n=NCOL, hooks={}):
                free = c[f"acc_free{pair}"]
                if first == 0 and free.n:
                    pe.wait_ge(free.sem, free.now())
                outs = [acc[pair][t][:, :] for t in range(NT)]
                for j in range(first, end):
                    block_products(j, KSB, COL, hi, lo, outs, P, n * KSB - 1)
                    for hook in hooks.get(j, ()):
                        hook()

            def start(pair, hi, lo, n=NCOL, count=1):
                column(pair, hi, lo, end=count, n=n)

            def rest(pair, hi, lo, n=NCOL, first=1, hooks={}):
                column(pair, hi, lo, first=first, end=n, n=n, hooks=hooks)

            def tp_wait():
                for b in range(2):
                    free = c[f"tp_free{b}"]
                    if free.n:
                        pe.wait_ge(free.sem, free.now())
                    free.more()

            def tp_settled():
                for b in range(2):
                    pe.wait_ge(S[f"tp_free{b}"], c[f"tp_free{b}"].now())

            def transpose_staging():
                pe.wait_ge(S["staging_full"], c.staging_full.more(2))
                tp_wait()
                for b in range(2):
                    for f in range(2):
                        for t in range(NT):
                            end = nc.tensor.transpose(
                                tp[b][:, f * SEQ + t * P:f * SEQ + (t + 1) * P],
                                staging[:, t, (2 * b + f) * P:(2 * b + f + 1) * P], ident[:, :])
                    end.then_inc(S[f"tp_ready{b}"], 1)

            pe.wait_ge(S["const_ready"], 1)
            for f in range(KT // 4):
                pe.wait_ge(S[f"x_landed{f}"], 16)
                tp_wait()
                for b in range(2):
                    for kk in range(2):
                        k = 4 * f + 2 * b + kk
                        for t in range(NT):
                            end = nc.tensor.transpose(tp[b][:, kk * SEQ + t * P:kk * SEQ + (t + 1) * P],
                                                      x_tok[:, t, k * P:(k + 1) * P], ident[:, :])
                    end.then_inc(S[f"tp_ready{b}"], 1)
                if f:
                    column(0, h_hi, h_lo, first=2 * f - 2, end=2 * f)
            tp_settled()
            column(0, h_hi, h_lo, first=NCOL - 2)

            def small_products():
                pe.wait_ge(S["const_ready"], 5)
                pe.wait_ge(S["ws_lo_ready"], 1)
                for t in range(NT):
                    rows = slice(t * P, (t + 1) * P)
                    o = mix[0][:, t * NSMALL:(t + 1) * NSMALL]
                    for k in range(KT):
                        nc.tensor.matmul(o, h_hi[:, k, rows], ws_hi[:, k, :], start=k == 0, stop=False)
                        nc.tensor.matmul(o, h_hi[:, k, rows], ws_lo[:, k, :], start=False, stop=False)
                        end = nc.tensor.matmul(o, h_lo[:, k, rows], ws_hi[:, k, :], start=False, stop=k == KT - 1)
                end.then_inc(S["small_ready"], 1)

            def low_rank_T():
                pe.wait_ge(S["z_small_ready"], NT)
                for t in range(NT):
                    end = nc.tensor.transpose(mix[1][0:GATE_RANK, t * P:(t + 1) * P],
                                              z_small[:, t, 0:GATE_RANK], ident[:, :])
                end.then_inc(S["glr_ready"], 1)

            for n in range(3):
                pair = (n + 1) % 2
                start(pair, h_hi, h_lo)
                transpose_staging()
                rest(pair, h_hi, h_lo, hooks={2: [small_products], 5: [low_rank_T]} if n == 0 else {})
            start(0, h_hi, h_lo)
            transpose_staging()
            rest(0, h_hi, h_lo)
            c.acc_free0.more(2)
            column(1, h_hi, h_lo)
            c.acc_free1.more(2)

            for n in range(2):
                pe.wait_ge(S["flat_lo_ready"], n + 1)
                if n == 0:
                    pe.wait_ge(S["glr_T_ready"], 1)
                for j in range(NCB):
                    block_products(j, 4, CMP_HIDDEN, flat_hi[n], flat_lo[n],
                                   [mix[n][0:NC4, 0:CMP_HIDDEN]], NC4, CMP_LEN - 1)

            def hidden_T():
                tp_settled()
                pe.wait_ge(S["hid_sb_ready"], 1)
                for n in range(2):
                    for k in range(2):
                        end = nc.tensor.transpose(tp[0][:, (2 * n + k) * 64:(2 * n + k) * 64 + NC4],
                                                  hid[:, n, k * P:(k + 1) * P], ident[0:NC4, 0:NC4])
                end.then_inc(S["hid_tp"], 1)

            def compressed():
                pe.wait_ge(S["hid_T_ready"], 1)
                for k in range(2):
                    nc.tensor.matmul(tp[1][:, 0:NC4], w2_sb[:, 0, k, :], hid_T[:, k, 0:NC4],
                                     start=k == 0, stop=k == 1)
                for g in range(KV_HEADS):
                    for k in range(2):
                        end = nc.tensor.matmul(mix[0][0:NCMP, g * HD:(g + 1) * HD],
                                               hid_T[:, 2 + k, g * NCMP:(g + 1) * NCMP], w2_sb[:, 1, k, :],
                                               start=k == 0, stop=k == 1)
                end.then_inc(S["cmp_out"], 1)

            gate_banks = [*tp, *mix]

            def decay_gates():
                pe.wait_ge(S["cmp_sb"], 2)
                for f in range(GLA_DK // P):
                    end = nc.tensor.matmul(gate_banks[f // 2][:, (f % 2) * SEQ:(f % 2 + 1) * SEQ],
                                           w_gate_sb[:, f * P:(f + 1) * P], glr_T[:, :], start=True, stop=True)
                end.then_inc(S["gate_mm"], 1)

            start(0, h_hi, h_lo)
            for n in range(4):
                rest(n % 2, h_hi, h_lo, hooks={2: [hidden_T], 3: [compressed], 4: [decay_gates]} if n == 0 else {})
                start((n + 1) % 2, h_hi, h_lo)
                if n == 0:
                    pe.wait_ge(S["gate_sb"], GLA_DK // P)
                transpose_staging()

            def token_major(trips):
                with c.loop(pe, trips, lo_ready=2 * NCOL, acc_free0=2, acc_free1=2):
                    rest(0, h_hi, h_lo)
                    c.acc_free0.more(2)
                    column(1, h_hi, h_lo)
                    c.acc_free1.more(2)
                    start(0, h_hi, h_lo)

            token_major(2)
            token_major(2)

            def gla_scores():
                pe.wait_ge(S["gla_ops"], c.gla_ops.more())
                for tile, kc, qc in ((0, 0, 0), (0, 0, 1), (0, 1, 1), (1, 0, 2), (1, 0, 3), (1, 1, 2),
                                     (1, 1, 3), (2, 2, 2), (2, 2, 3), (2, 3, 3)):
                    row = (kc % 2) * CHUNK
                    col = tile * P + (qc % 2) * CHUNK
                    o = mix[0][row:row + CHUNK, col:col + CHUNK]
                    for f in range(FT):
                        keys = (e_neg if kc == qc else e_end)[:, f, kc, :]
                        queries = (q_dec[:, f, qc, :] if qc - kc <= 1 else
                                   q2[:, f, qc - 2, :] if qc - kc == 2 else q3[:, f, :])
                        end = nc.tensor.matmul(o, keys, queries, start=f == 0, stop=f == FT - 1)
                end.then_inc(S["gla_attn"], 1)

            def gla_values(i):
                def go():
                    pe.wait_ge(S["attn_ready"], c.attn_ready.more())
                    nc.tensor.matmul(mix[0][:, :], attn_sb[:, 0, :], gv[:, i, 0, :], start=True, stop=True)
                    nc.tensor.matmul(mix[1][:, :], attn_sb[:, 1, :], gv[:, i, 0, :], start=True, stop=False)
                    nc.tensor.matmul(mix[1][:, :], attn_sb[:, 2, :], gv[:, i, 1, :], start=False,
                                     stop=True).then_inc(S["gla_o_ready"], 1)
                return go

            with c.loop(pe, GLA_HEADS // 2, lo_ready=2 * NCOL, gla_ops=2, attn_ready=2, tp_free0=4, tp_free1=4,
                        staging_full=8) as i:
                for n in range(2):
                    rest(n, h_hi, h_lo, hooks={4: [gla_scores], 5: [gla_values(i * 2 + n)], 7: [transpose_staging]})
                    start(1 - n, h_hi, h_lo)
                    transpose_staging()

            def cmp_scores(i):
                def go():
                    pe.wait_ge(S["q_st_ready"], c.q_st_ready.more())
                    pe.wait_ge(S["v_st_ready"], c.v_st_ready.more())
                    tp_settled()
                    for u in range(GROUP):
                        for t in range(NT):
                            at_col = (u * NT + t) * STRIDE
                            end = nc.tensor.matmul(tp[1][:, at_col:at_col + NCMP], q_st[:, u, t * P:(t + 1) * P],
                                                   k_cmp_T[:, bass.ds(i * NCMP, NCMP)], start=True, stop=True)
                    end.then_inc(S["cs_ready"], 1)
                return go

            def scores(i, u):
                def go():
                    nc.tensor.matmul(mix[0][:, 0:SEQ], q_st[:, u, 0:P], ksw_T[:, :, i, 0:P],
                                     start=True, stop=True)
                    nc.tensor.matmul(mix[1][:, :], q_st[:, u, P:SEQ], ksw_T[:, :, i, :], start=True,
                                     stop=True).then_inc(S["qk_ready"], 1)
                return go

            def probs_T(u):
                def go():
                    pe.wait_ge(S["p_ready"], c.p_ready.more())
                    if u:
                        pe.wait_ge(S["on_ready"], c.on_ready.now())
                    tp_wait()
                    for n in range(2):
                        nc.tensor.transpose(tp[n][:, 0:P], p_sc[:, n * P:(n + 1) * P], ident[:, :])
                        for k in range(NT):
                            off = SEQ + n * SEQ + k * P
                            nc.tensor.transpose(tp[n][:, (1 + k) * P:(2 + k) * P], p_sc[:, off:off + P],
                                                ident[:, :])
                        nc.tensor.transpose(tp[n][0:NCMP, 3 * P:4 * P], p_c[:, u, n, 0:NCMP],
                                            ident[:, :]).then_inc(S[f"tp_ready{n}"], 1)
                return go

            def outputs(u):
                def go():
                    tp_settled()
                    c.on_ready.more()
                    o, late = tp[0][:, 0:SEQ], tp[0][:, P:SEQ]
                    nc.tensor.matmul(o, v_st[:, 0, 0, :], p_T[:, 0, 0:SEQ], start=True, stop=False)
                    nc.tensor.matmul(o, v_st[:, 1, 0, :], p_T[:, 1, 0:SEQ], start=False, stop=False)
                    nc.tensor.matmul(o, vc_st[:, :], p_T[0:NCMP, :, SEQ + P:2 * SEQ], start=False, stop=False)
                    nc.tensor.matmul(late, v_st[:, 0, 1, :], p_T[:, 0, SEQ:SEQ + P], start=False, stop=False)
                    nc.tensor.matmul(late, v_st[:, 1, 1, :], p_T[:, 1, SEQ:SEQ + P], start=False,
                                     stop=True).then_inc(S["pv_ready"], 1)
                return go

            tp_settled()
            with c.loop(pe, KV_HEADS, lo_ready=2 * NCOL, acc_free0=2, acc_free1=2, tp_free0=4, tp_free1=4,
                        q_st_ready=1, v_st_ready=1, on_ready=4, p_ready=4) as i:
                rest(0, h_hi, h_lo, hooks={1: [cmp_scores(i), scores(i, 0)], 4: [probs_T(0), scores(i, 1)],
                                           5: [outputs(0)], 7: [probs_T(1), scores(i, 2)]})
                c.acc_free0.more(2)
                column(1, og_hi, og_lo, hooks={0: [outputs(1)], 2: [probs_T(2), scores(i, 3)], 3: [outputs(2)],
                                               5: [probs_T(3)], 6: [outputs(3)]})
                c.acc_free1.more(2)
                start(0, h_hi, h_lo)
                pe.wait_ge(S["on_ready"], c.on_ready.now())

            def merge(hi, lo):
                rest(0, h_hi, h_lo, first=2)
                c.acc_free0.more(2)
                pe.wait_ge(S["on_lo_ready"], 4)
                column(1, on_hi, on_lo)
                c.acc_free1.more(2)
                start(0, hi, lo, count=2)
                transpose_staging()

            column(0, h_hi, h_lo, first=1, end=2)
            with c.loop(pe, 3, lo_ready=2 * NCOL, acc_free0=2, acc_free1=2, tp_free0=1, tp_free1=1,
                        staging_full=2):
                merge(h_hi, h_lo)
            merge(m_hi, m_lo)

            for n in range(4):
                rest(n % 2, m_hi, m_lo, first=2 if n == 0 else 1, hooks={5: [tp_settled]} if n == 0 else {})
                if n < 3:
                    start((n + 1) % 2, m_hi, m_lo)
                else:
                    start(0, f_hi, f_lo)
                transpose_staging()

            def gated(hi, lo, n):
                rest(0, f_hi, f_lo, hooks={5: [tp_settled]})
                c.acc_free0.more(2)
                column(1, f_hi, f_lo)
                start(0, hi, lo, n)
                transpose_staging()

            with c.loop(pe, FFB - 1, lo_ready=2 * NCOL, acc_free0=2, tp_free0=1, tp_free1=1, staging_full=2):
                gated(f_hi, f_lo, NCOL)
            gated(act_hi, act_lo, NDOWN)
            for n in range(4):
                if n:
                    start(n % 2, act_hi, act_lo, NDOWN)
                rest(n % 2, act_hi, act_lo, NDOWN, hooks={NDOWN - 3: [tp_settled]} if n == 0 else {})
                c[f"acc_free{n % 2}"].more(2)

        SPLITS = {n: 16 * NCOL // SLOTS for n in ("raw_landed0", "raw_landed1", "raw_landed2", "raw_landed3")}

        @block.scalar
        def _(act):
            c = Counts(S)
            LOOP = dict(SPLITS, hi_ready=NCOL, block_done=NCOL)
            LOOP2 = {n: 2 * v for n, v in LOOP.items()}

            def split():
                s = c.hi_ready.n % SLOTS
                landed = c[f"raw_landed{s}"]
                act.wait_ge(landed.sem, landed.more(16))
                c.hi_ready.more()
                if c.hi_ready.n > SLOTS:
                    act.wait_ge(S["block_done"], c.hi_ready.now(SLOTS))
                nc.scalar.activation(w_hi[s][:, :], w_raw[s][:, :], ACT.Copy).then_inc(S["hi_ready"], 1)

            def blocks(n=NCOL, first=0, hooks={}, splits=None):
                for j in range(first, n):
                    if splits is None or j < splits:
                        split()
                    for hook in hooks.get(j, ()):
                        hook()
                c.block_done.more(n - first)

            def summed():
                act.wait_ge(S["block_done"], c.block_done.now())

            def step(ins):
                ins.then_inc(S["act_step"], 1)
                act.wait_ge(S["act_step"], c.act_step.more())

            def root():
                act.wait_ge(S["ms_ready"], c.ms_ready.more())
                nc.scalar.activation(rs[:, :], ms[:, :], ACT.Sqrt).then_inc(S["root_ready"], 1)

            def square_sum(src, o, junk):
                if c.sumsq_ready.n:
                    act.wait_ge(S["sumsq_ready"], c.sumsq_ready.now())
                c.sumsq_ready.more()
                nc.scalar.activation(junk, src, ACT.Square, accum_out=o).then_inc(S["sumsq_ready"], 1)

            act.dma_start(par[:, :], params).then_inc(S["par_landed"], 16)

            act.wait_ge(S["par_landed"], 16)
            for f in range(KT // 4):
                for b in range(2):
                    act.wait_ge(S[f"tp_ready{b}"], c[f"tp_ready{b}"].more())
                    for kk in range(2):
                        k = 4 * f + 2 * b + kk
                        nc.scalar.activation(h_hi[:, k, :], tp[b][:, kk * SEQ:(kk + 1) * SEQ], ACT.Copy,
                                             scale=par[:, C_GMIX + k:C_GMIX + k + 1]).then_inc(S["tp_hi"], 1)
                split()
                split()
                if f == 1:
                    act.dma_start(ws_raw[:, :, :], wsmall).then_inc(S["small_landed"], 16)
                    act.dma_start(w_gate_sb[:, :], w_gate).then_inc(S["small_landed"], 16)
                    act.dma_start(w2_sb[:, :, :, :], w2).then_inc(S["small_landed"], 16)
                    act.dma_start(g_gla_bc[:, :], g_gla.broadcast_to([P, HV])).then_inc(S["small_landed"], 16)
            c.tp_hi.more(KT)
            for t in range(NT):
                square_sum(x_tok[:, t, :], sumsq[:, t, 0:1], square_junk[:, :])
                split()
            root()
            split()
            c.block_done.more(NCOL)
            act.wait_ge(S["rs_ready"], 1)

            def stage_tile(pair):
                summed()
                for b in range(2):
                    act.wait_ge(S[f"tp_ready{b}"], c[f"tp_ready{b}"].now())
                nc.scalar.activation(staging[:, 0, :], acc[pair][0][:, :], ACT.Copy, scale=rs_h[:, 0:1]).then_inc(
                    S["staging_full"], 1)
                c.staging_full.more(2)

            def store_T(dest):
                act.wait_ge(S["tp_ready0"], c.tp_ready0.more())
                c.tp_ready1.more()
                nc.scalar.activation(dest[:, 0:2, :], tp[0][:, :].rearrange("p (f s) -> p f s", f=2),
                                     ACT.Copy).then_inc(S["tp_free0"], 1)

            def small_hi():
                act.wait_ge(S["small_landed"], 64)
                nc.scalar.activation(ws_hi[:, :, :], ws_raw[:, :, :], ACT.Copy).then_inc(S["ws_hi_ready"], 1)

            def small_gates():
                act.wait_ge(S["small_ready"], 1)
                for t in range(NT):
                    nc.scalar.activation(z_small[:, t, :], mix[0][:, t * NSMALL:(t + 1) * NSMALL], ACT.Copy,
                                         scale=rs_h[:, t:t + 1]).then_inc(S["z_small_ready"], 1)
                act.wait_ge(S["z_small_ready"], NT)
                nc.scalar.activation(branch_gate[:, :, :, :].rearrange("p t n h -> p t (n h)"),
                                     z_small[:, :, GATE_RANK:NSMALL], ACT.Sigmoid).then_inc(
                                         S["branch_gate_ready"], 1)

            def low_rank_T():
                act.wait_ge(S["glr_ready"], 1)
                nc.scalar.activation(glr_T[:, :], mix[1][0:GATE_RANK, 0:SEQ], ACT.Copy).then_inc(
                    S["glr_T_ready"], 1)

            def copy_tile(dest, pair):
                summed()
                nc.scalar.activation(dest, acc[pair][0][:, :], ACT.Copy, scale=rs_h[:, 0:1]).then_inc(
                    S[f"acc_free{pair}"], 1)

            def flat_split(n):
                act.wait_ge(S["flat_ready"], 2 * (n + 1))
                nc.scalar.activation(flat_hi[n][:, :, :], flat[n][:, :, :, :].rearrange("p l h j -> p l (h j)"),
                                     ACT.Copy).then_inc(S["flat_hi_ready"], 1)

            stage_tile(0)
            for n, (dest, hooks) in enumerate((
                    (kvc_T[:, 0, :, :], {1: [small_hi], 3: [small_gates], 5: [low_rank_T], 6: [lambda: flat_split(0)]}),
                    (kvc_T[:, 1, :, :], {4: [lambda: flat_split(1)]}),
                    (ksw_T[:, 0, :, :], {}))):
                blocks(1)
                store_T(dest)
                blocks(first=1, hooks=hooks)
                stage_tile((n + 1) % 2)
            blocks(1)
            store_T(ksw_T[:, 1, :, :])
            blocks(first=1)
            copy_tile(vsw[:, 0, 0, :], 0)
            blocks()
            copy_tile(vsw[:, 1, 0, :], 1)

            blocks()
            blocks()

            def hidden_gate():
                for n in range(2):
                    nc.scalar.activation(hid_gate[:, n, :], mix[n][0:NC4, 0:CMP_HIDDEN], ACT.Sigmoid).then_inc(
                        S["hid_gate_ready"], 1)

            def hidden_T():
                act.wait_ge(S["hid_tp"], 1)
                nc.scalar.activation(hid_T[:, :, 0:NC4], tp[0][:, 0:256].rearrange("p (a n) -> p a n", a=4)[:, :, 0:NC4],
                                     ACT.Copy).then_inc(S["hid_T_ready"], 1)

            def compressed():
                act.wait_ge(S["cmp_out"], 1)
                nc.scalar.activation(k_cmp_T[:, :], tp[1][:, 0:NC4], ACT.Copy).then_inc(S["cmp_sb"], 1)

            def log_exp():
                act.wait_ge(S["nega_ready"], 1)
                step(nc.scalar.activation(log_a[:, :], log_a[:, :], ACT.Exp))

            def log_1p():
                nc.scalar.activation(log_a[:, :], log_a[:, :], ACT.Ln, bias=1.0).then_inc(S["ln_ready"], 1)

            summed()
            blocks(1)
            for n in range(4):
                blocks(first=1, hooks=({1: [hidden_gate], 2: [hidden_T], 3: [compressed]},
                                       {1: [log_exp], 3: [log_1p]}, {}, {})[n])
                stage_tile(n % 2)
                blocks(1)
                store_T(gqk_blocks[:, n, :, :])

            with c.loop(act, 2, **LOOP2) as i:
                blocks(first=1)
                copy_tile(gv[:, i * 2, 0, :], 0)
                blocks()
                copy_tile(gv[:, i * 2 + 1, 0, :], 1)
                blocks(1)
            with c.loop(act, 2, **LOOP2) as i:
                for n in range(2):
                    blocks(first=1 - n)
                    summed()
                    for t in range(NT):
                        nc.scalar.activation(r_gate[n][:, t, :], acc[n][t][:, :], ACT.Sigmoid,
                                             scale=rs_h[:, t:t + 1]).then_inc(S["gr_gate"], 1)
                blocks(1)

            def gla_exps(i):
                def go():
                    nc.scalar.activation(e_pos[:, :, :, :].rearrange("p f n c -> p (f n) c"),
                                         decay_sum[:, i, :, :], ACT.Exp, scale=1.0 / TAU)
                    nc.scalar.activation(e_neg[:, :, :, :].rearrange("p f n c -> p (f n) c"),
                                         decay_sum[:, i, :, :], ACT.Exp, scale=-1.0 / TAU)
                return go

            def gla_exp_end():
                act.wait_ge(S["decay_ready"], c.decay_ready.more())
                nc.scalar.activation(e_end[:, :, :, :], e_end[:, :, :, :], ACT.Exp,
                                     scale=1.0 / TAU).then_inc(S["exp_ready"], 1)

            def gla_squares():
                act.wait_ge(S["gla_o_ready"], c.gla_o_ready.more())
                for t in range(NT):
                    square_sum(mix[t][:, :], sumsq[:, t, 0:1], e_pos[:, :, :, :].rearrange("p f n c -> p (f n c)"))
                c.staging_full.more(2)

            def tp_split(hi, scales=None):
                for b in range(2):
                    act.wait_ge(S[f"tp_ready{b}"], c[f"tp_ready{b}"].more())
                    if scales is None:
                        nc.scalar.activation(hi[:, 2 * b:2 * b + 2, :], tp[b][:, :].rearrange("p (f s) -> p f s", f=2),
                                             ACT.Copy).then_inc(S["tp_hi"], 1)
                    else:
                        for f in range(2):
                            nc.scalar.activation(hi[:, 2 * b + f, :], tp[b][:, f * SEQ:(f + 1) * SEQ], ACT.Copy,
                                                 scale=scales(2 * b + f)).then_inc(S["tp_hi"], 1)

            with c.loop(act, GLA_HEADS // 2, **dict(LOOP2, tp_ready0=4, tp_ready1=4, staging_full=8, decay_ready=2,
                                                    gla_o_ready=2, ms_ready=2, sumsq_ready=4)) as i:
                for n in range(2):
                    head = i * 2 + n
                    blocks(first=1, hooks={1: [gla_exps(head)], 2: [gla_exp_end], 5: [gla_squares, root],
                                           7: [lambda: tp_split(blocks_of(og_hi)[:, head, :, :])]})
                    stage_tile(n)
                    blocks(1)
                    store_T(nq_T[:, head, :, :])

            def cmp_exp():
                act.wait_ge(S["cs_sub"], c.cs_sub.more())
                nc.scalar.activation(p_c[:, :, :, 0:NCMP], p_c[:, :, :, 0:NCMP], ACT.Exp).then_inc(S["cs_exp"], 1)

            def exps():
                act.wait_ge(S["nmax_ready"], c.nmax_ready.more())
                for t in range(NT):
                    for n in range(2):
                        at_col, width = (n * P, P) if t == 0 else (SEQ + n * SEQ, SEQ)
                        part = p_sc[:, at_col:at_col + width]
                        end = nc.scalar.activation(part, part, ACT.Exp, bias=nmax[:, t, n:n + 1],
                                                   accum_out=coef[:, t, n:n + 1])
                end.then_inc(S["p_exp"], 1)

            def store_p():
                act.wait_ge(S["tp_ready0"], c.tp_ready0.more())
                c.tp_ready1.more()
                nc.scalar.activation(p_T[:, 0, 0:3 * P], tp[0][:, 0:3 * P], ACT.Copy)
                nc.scalar.activation(p_T[0:NCMP, 0, 3 * P:4 * P], tp[0][0:NCMP, 3 * P:4 * P],
                                     ACT.Copy).then_inc(S["tp_free0"], 1)

            def store_o(i, u):
                def go():
                    act.wait_ge(S["pv_ready"], c.pv_ready.more())
                    nc.scalar.activation(on_T[:, i, u, :], tp[0][:, 0:SEQ], ACT.Copy).then_inc(
                        S["on_ready"], 1)
                return go

            def merge_gate():
                summed()
                for t in range(NT):
                    nc.scalar.activation(gate[:, t, :], acc[0][t][:, :], ACT.Sigmoid, scale=rs_h[:, t:t + 1]).then_inc(
                        S["acc_free0"], 1)

            with c.loop(act, KV_HEADS, **dict(LOOP2, tp_ready0=4, tp_ready1=4, cs_sub=1, nmax_ready=4,
                                              pv_ready=4)) as i:
                blocks(first=1, hooks={2: [cmp_exp, exps], 4: [store_p], 5: [exps], 6: [store_o(i, 0)], 7: [store_p]})
                merge_gate()
                blocks(hooks={0: [exps], 1: [store_o(i, 1)], 2: [store_p], 3: [exps], 4: [store_o(i, 2)], 5: [store_p],
                              7: [store_o(i, 3)]})
                summed()
                blocks(1)

            act.wait_ge(S["on_ready"], HEADS)
            for t in range(NT):
                act.dma_start(x1[:, t, :], x[t]).then_inc(S["xres_landed"], 16)

            def on_chunk(n):
                return lambda: nc.scalar.activation(on_hi[:, 4 * n:4 * n + 4, :], on_T[:, n, :, :],
                                                    ACT.Copy).then_inc(S["on_hi_ready"], 1)

            blocks(2, first=1)
            for begin, trips in ((0, 1), (1, 2), (3, 1)):
                with c.loop(act, trips, **dict(LOOP2, tp_ready0=1, tp_ready1=1, staging_full=2)) as i:
                    blocks(first=2, hooks={(2, 3, 5, 6)[n]: [on_chunk(n)] for n in range(4)} if begin == 0 else {})
                    merge_gate()
                    blocks()
                    c.staging_full.more(2)
                    blocks(2)
                    tp_split(blocks_of(m_hi)[:, begin if trips == 1 else i + begin, :, :])

            for i in range(4):
                blocks(first=2 if i == 0 else 1)
                act.wait_ge(S["staging_full"], c.staging_full.more(2))
                nc.scalar.activation(x1[:, :, i * COL:(i + 1) * COL], staging[:, :, :], ACT.Copy)
                for t in range(NT):
                    square_sum(staging[:, t, :], sumsq[:, t, i:i + 1], mix[0][:, :])
                if i == 3:
                    root()
                blocks(1)
                tp_split(blocks_of(f_hi)[:, i, :, :], lambda f: par[:, C_GFFN + 4 * i + f:C_GFFN + 4 * i + f + 1])
            act.dma_start(g_fin_bc[:, :], g_final.broadcast_to([P, D])).then_inc(S["gfin_landed"], 16)

            act.wait_ge(S["rs_ready"], 2)
            with c.loop(act, FFB, **dict(LOOP2, tp_ready0=1, tp_ready1=1)) as i:
                blocks(first=1)
                summed()
                for t in range(NT):
                    nc.scalar.activation(ffn_gate[:, t, :], acc[0][t][:, :], ACT.Sigmoid,
                                         scale=rs[:, t:t + 1]).then_inc(S["gate_ready"], 1)
                blocks()
                blocks(1)
                tp_split(act_hi[:, :, :].rearrange("p (a f) s -> p a f s", f=4)[:, i, :, :])
            c.acc_free0.more(2 * (5 + 4 + 4 + FFB))
            c.acc_free1.more(2 * (5 + 4 + 4))
            step(nc.scalar.activation(rs_t[:, :], ms[:, :], ACT.Sqrt))
            for n in range(4):
                blocks(NDOWN, first=1 if n == 0 else 0, splits=NDOWN if n < 3 else NDOWN - LEAD)
                for t in range(NT):
                    added = c[f"acc_free{n % 2}"]
                    act.wait_ge(added.sem, added.more())
                    square_sum(x1[:, t, n * COL:(n + 1) * COL], sumsq[:, t, n:n + 1], mix[0][:, :])
            root()

        @block.vector
        def _(dve):
            c = Counts(S)
            LOOP = dict(lo_ready=NCOL, block_done=NCOL)
            LOOP2 = {n: 2 * v for n, v in LOOP.items()}

            def split():
                s = c.lo_ready.n % SLOTS
                dve.wait_ge(S["hi_ready"], c.lo_ready.more())
                nc.vector.tensor_tensor(w_lo[s][:, :], w_raw[s][:, :], f32(w_hi[s][:, :]),
                                        ALU.subtract).then_inc(S["lo_ready"], 1)

            def blocks(n=NCOL, first=0, hooks={}, splits=None):
                for j in range(first, n):
                    if splits is None or j < splits:
                        split()
                    for hook in hooks.get(j, ()):
                        hook()
                c.block_done.more(n - first)

            def summed():
                dve.wait_ge(S["block_done"], c.block_done.now())

            def step(ins):
                ins.then_inc(S["dve_step"], 1)
                dve.wait_ge(S["dve_step"], c.dve_step.more())

            def mean_squares(src, n):
                nc.vector.tensor_scalar(ms[:, :], src, 1.0 / n, EPS, ALU.mult, ALU.add).then_inc(S["ms_ready"], 1)

            def reciprocal_root():
                dve.wait_ge(S["root_ready"], c.root_ready.more())
                step(nc.vector.reciprocal(rs[:, :], rs[:, :]))
                step(nc.vector.tensor_tensor(rs_t[:, :], rs[:, :], rs[:, :], ALU.mult))
                step(nc.vector.tensor_tensor(rs_t[:, :], rs_t[:, :], ms[:, :], ALU.mult))
                step(nc.vector.tensor_scalar(rs_t[:, :], rs_t[:, :], -0.5, 1.5, ALU.mult, ALU.add))
                step(nc.vector.tensor_tensor(rs[:, :], rs[:, :], rs_t[:, :], ALU.mult))

            def sum_waits(n=NT):
                dve.wait_ge(S["sumsq_ready"], c.sumsq_ready.more(n))

            for f in range(KT // 4):
                for b in range(2):
                    c[f"tp_ready{b}"].more()
                    dve.wait_ge(S["tp_hi"], c.tp_hi.more(2))
                    for kk in range(2):
                        k = 4 * f + 2 * b + kk
                        end = nc.vector.scalar_tensor_tensor(
                            h_lo[:, k, :], tp[b][:, kk * SEQ:(kk + 1) * SEQ], par[:, C_GMIX + k:C_GMIX + k + 1],
                            f32(h_hi[:, k, :]), ALU.mult, ALU.subtract)
                    end.then_inc(S[f"tp_free{b}"], 1)
                split()
                split()
            for t in range(NT):
                split()
            sum_waits()
            mean_squares(sumsq[:, :, 0], D)
            reciprocal_root()
            nc.vector.tensor_copy(rs_h[:, :], rs[:, :]).then_inc(S["rs_ready"], 1)
            split()
            c.block_done.more(NCOL)
            dve.wait_ge(S["rs_ready"], 1)

            def small_lo():
                dve.wait_ge(S["ws_hi_ready"], 1)
                nc.vector.tensor_tensor(ws_lo[:, :, :], ws_raw[:, :, :], f32(ws_hi[:, :, :]),
                                        ALU.subtract).then_inc(S["ws_lo_ready"], 1)

            def staging_free():
                for b in range(2):
                    dve.wait_ge(S[f"tp_ready{b}"], c[f"tp_ready{b}"].now())

            def stage_tile(pair):
                summed()
                staging_free()
                nc.vector.tensor_scalar(staging[:, 1, :], acc[pair][1][:, :], rs_h[:, 1:2], None,
                                        ALU.mult).then_inc(S["staging_full"], 1)

            def store_T(dest):
                c.tp_ready0.more()
                dve.wait_ge(S["tp_ready1"], c.tp_ready1.more())
                nc.vector.tensor_copy(dest[:, 2:4, :], tp[1][:, :].rearrange("p (f s) -> p f s", f=2)).then_inc(
                    S["tp_free1"], 1)

            def stored():
                for b in range(2):
                    dve.wait_ge(S[f"tp_free{b}"], c[f"tp_ready{b}"].now())

            def copy_tile(dest, pair):
                summed()
                nc.vector.tensor_scalar(dest, acc[pair][1][:, :], rs_h[:, 1:2], None, ALU.mult).then_inc(
                    S[f"acc_free{pair}"], 1)

            def flatten_blocks(n):
                stored()
                col = (C_PEK, C_PEV)[n]
                for half in range(2):
                    tokens = kvc_T[:, n, :, half * STRIDE:half * STRIDE + NCMP * STRIDE]
                    src = tokens.rearrange("p h (j l) -> p l h j", l=STRIDE)
                    pe_cols = par[:, col + half * STRIDE:col + (half + 1) * STRIDE]
                    pe_all = pe_cols.rearrange("p (l a b) -> p l a b", a=1, b=1).broadcast_to(
                        [P, STRIDE, KV_HEADS, NCMP])
                    nc.vector.tensor_tensor(flat[n][:, half * STRIDE:(half + 1) * STRIDE, :, :], src, pe_all,
                                            ALU.add).then_inc(S["flat_ready"], 1)

            def flatten_lo(n):
                dve.wait_ge(S["flat_hi_ready"], n + 1)
                nc.vector.tensor_tensor(flat_lo[n][:, :, :], flat[n][:, :, :, :].rearrange("p l h j -> p l (h j)"),
                                        f32(flat_hi[n][:, :, :]), ALU.subtract).then_inc(S["flat_lo_ready"], 1)

            stage_tile(0)
            for n, (dest, hooks) in enumerate((
                    (kvc_T[:, 0, :, :], {1: [small_lo], 4: [lambda: flatten_blocks(0)], 7: [lambda: flatten_lo(0)]}),
                    (kvc_T[:, 1, :, :], {2: [lambda: flatten_blocks(1)], 5: [lambda: flatten_lo(1)]}),
                    (ksw_T[:, 0, :, :], {}))):
                blocks(1)
                store_T(dest)
                blocks(first=1, hooks=hooks)
                stage_tile((n + 1) % 2)
            blocks(1)
            store_T(ksw_T[:, 1, :, :])
            blocks(first=1)
            copy_tile(vsw[:, 0, 1, :], 0)
            blocks()
            copy_tile(vsw[:, 1, 1, :], 1)

            blocks()
            blocks()

            def hidden():
                dve.wait_ge(S["hid_gate_ready"], 2)
                for n in range(2):
                    end = nc.vector.tensor_tensor(hid[:, n, :], mix[n][0:NC4, 0:CMP_HIDDEN], hid_gate[:, n, :], ALU.mult)
                end.then_inc(S["hid_sb_ready"], 1)

            def compressed():
                dve.wait_ge(S["cmp_out"], 1)
                nc.vector.tensor_copy(v_cmp[:, :, :],
                                      mix[0][0:NCMP, :].rearrange("p (g d) -> p g d", g=KV_HEADS)).then_inc(
                                          S["cmp_sb"], 1)

            gate_banks = [*tp, *mix]
            a_all = decay_sum[:, :, :, :].rearrange("p h n c -> p (h n c)")

            def decay_gates():
                dve.wait_ge(S["gate_mm"], 1)
                for f in range(GLA_DK // P):
                    nc.vector.tensor_scalar(a_all[:, f * SEQ:(f + 1) * SEQ],
                                            gate_banks[f // 2][:, (f % 2) * SEQ:(f % 2 + 1) * SEQ],
                                            par[:, C_BG + f:C_BG + f + 1], None, ALU.add).then_inc(S["gate_sb"], 1)

            def negative():
                dve.wait_ge(S["gate_sb"], GLA_DK // P)
                nc.vector.scalar_tensor_tensor(log_a[:, :], a_all, -1.0, a_all, ALU.mult, ALU.min).then_inc(
                    S["nega_ready"], 1)

            def log_decay():
                dve.wait_ge(S["ln_ready"], 1)
                step(nc.vector.scalar_tensor_tensor(log_a[:, :], a_all, 0.0, log_a[:, :], ALU.min, ALU.subtract))

            def decay_sums():
                dve.wait_ge(S["keep_ready"], 1)
                step(nc.vector.tensor_tensor_scan(a_all, chunk_keep[:, :], log_a[:, :], 0.0, ALU.mult, ALU.add))

            blocks(1)
            for n in range(4):
                blocks(first=1, hooks=({1: [hidden], 3: [compressed], 5: [decay_gates], 6: [negative]},
                                       {5: [log_decay]}, {3: [decay_sums]}, {})[n])
                stage_tile(n % 2)
                blocks(1)
                store_T(gqk_blocks[:, n, :, :])

            with c.loop(dve, 2, **LOOP2) as i:
                blocks(first=1)
                copy_tile(gv[:, i * 2, 1, :], 0)
                blocks()
                copy_tile(gv[:, i * 2 + 1, 1, :], 1)
                blocks(1)
            with c.loop(dve, 2, **dict(LOOP2, gr_gate=4, dve_step=2)) as i:
                for n in range(2):
                    blocks(first=1 - n)
                    dve.wait_ge(S["gr_gate"], c.gr_gate.more(2))
                    r = r_gate[n][:, :, :]
                    gain = g_gla_bc[:, :].rearrange("p (a n) -> p a n", a=1).broadcast_to([P, NT, HV])
                    step(nc.vector.tensor_tensor(r, r, gain, ALU.mult))
                    for t in range(NT):
                        nc.vector.scalar_tensor_tensor(gr[:, i * 2 + n, t, :], acc[n][t][:, :], rs_h[:, t:t + 1],
                                                       r[:, t, :], ALU.mult, ALU.mult).then_inc(
                                                           S[f"acc_free{n}"], 1)
                blocks(1)

            def gla_decays(i):
                def go():
                    b = decay_sum[:, i, :, :]
                    last = decay_sum[:, i, :, CHUNK - 1:CHUNK].broadcast_to([P, FT * NCH, CHUNK])
                    nc.vector.tensor_tensor(e_end[:, :, :, :].rearrange("p f n c -> p (f n) c"), last, b,
                                            ALU.subtract).then_inc(S["decay_ready"], 1)
                return go

            def gla_ops(i):
                def go():
                    dve.wait_ge(S["exp_ready"], c.exp_ready.more())
                    flat4 = "p f n c -> p (f n c)"
                    q = gqk_T[:, 0, i, :, :].rearrange("p f s -> p (f s)")
                    k = gqk_T[:, 1, i, :, :].rearrange("p f s -> p (f s)")
                    ep, en, ee, qd = (v[:, :, :, :].rearrange(flat4) for v in (e_pos, e_neg, e_end, q_dec))
                    nc.vector.tensor_tensor(en, k, en, ALU.mult)
                    nc.vector.tensor_tensor(ee, k, ee, ALU.mult)
                    step(nc.vector.scalar_tensor_tensor(qd, q, float(HK) ** -0.5, ep, ALU.mult, ALU.mult))
                    step(nc.vector.tensor_tensor(
                        q2[:, :, :, :], q_dec[:, :, 2:4, :],
                        e_pos[:, :, 1:3, CHUNK - 1:CHUNK].broadcast_to([P, FT, 2, CHUNK]), ALU.mult))
                    nc.vector.tensor_tensor(
                        q3[:, :, :], q2[:, :, 1, :],
                        e_pos[:, :, 1, CHUNK - 1:CHUNK].broadcast_to([P, FT, CHUNK]), ALU.mult).then_inc(
                            S["gla_ops"], 1)
                return go

            def gla_mask():
                dve.wait_ge(S["gla_attn"], c.gla_attn.more())
                nc.vector.tensor_copy(attn_sb[:, 1, :], mix[0][:, P:2 * P])
                for tile in (0, 2):
                    for row in (0, CHUNK):
                        rows = slice(row, row + CHUNK)
                        end = nc.vector.copy_predicated(
                            attn_sb[rows, tile, row:P], gla_valid[rows, row:P].bitcast(I32),
                            mix[0][rows, tile * P + row:(tile + 1) * P])
                end.then_inc(S["attn_ready"], 1)

            def gla_mean():
                sum_waits()
                mean_squares(sumsq[:, :, 0], HV)

            def gla_norm(i):
                def go():
                    reciprocal_root()
                    staging_free()
                    for t in range(NT):
                        nc.vector.scalar_tensor_tensor(staging[:, t, :], mix[t][:, :], rs[:, t:t + 1],
                                                       gr[:, i, t, :], ALU.mult, ALU.mult).then_inc(
                                                           S["staging_full"], 1)
                return go

            def tp_split(hi, lo, scales=None):
                for b in range(2):
                    c[f"tp_ready{b}"].more()
                    if scales is None:
                        dve.wait_ge(S["tp_hi"], c.tp_hi.more())
                        end = nc.vector.tensor_tensor(lo[:, 2 * b:2 * b + 2, :],
                                                      tp[b][:, :].rearrange("p (f s) -> p f s", f=2),
                                                      f32(hi[:, 2 * b:2 * b + 2, :]), ALU.subtract)
                    else:
                        dve.wait_ge(S["tp_hi"], c.tp_hi.more(2))
                        for f in range(2):
                            end = nc.vector.scalar_tensor_tensor(
                                lo[:, 2 * b + f, :], tp[b][:, f * SEQ:(f + 1) * SEQ], scales(2 * b + f),
                                f32(hi[:, 2 * b + f, :]), ALU.mult, ALU.subtract)
                    end.then_inc(S[f"tp_free{b}"], 1)

            with c.loop(dve, GLA_HEADS // 2, **dict(LOOP2, tp_ready0=4, tp_ready1=4, tp_hi=4, exp_ready=2, gla_attn=2,
                                                    sumsq_ready=4, root_ready=2, dve_step=14)) as i:
                for n in range(2):
                    head = i * 2 + n
                    blocks(first=1, hooks={1: [gla_decays(head)], 3: [gla_ops(head)], 4: [gla_mask],
                                           5: [gla_mean, gla_norm(head)],
                                           7: [lambda: tp_split(blocks_of(og_hi)[:, head, :, :],
                                                                blocks_of(og_lo)[:, head, :, :])]})
                    stage_tile(n)
                    blocks(1)
                    store_T(nq_T[:, head, :, :])

            def per_query(v):
                return v[:, :, 0:NCMP].rearrange("p (a t) c -> p a t c", a=1).broadcast_to([P, GROUP, NT, NCMP])

            def per_key(v):
                return v[:, :, :].rearrange("p u (t a) -> p u t a", a=1).broadcast_to([P, GROUP, NT, NCMP])

            pc = p_c[:, :, :, 0:NCMP]

            def cmp_max():
                dve.wait_ge(S["cs_ready"], c.cs_ready.more())
                cs = tp[1][:, 0:GROUP * NT * STRIDE].rearrange("p (u t c) -> p u t c", u=GROUP, t=NT)
                step(nc.vector.tensor_tensor(pc, cs[:, :, :, 0:NCMP], per_query(cmp_bias), ALU.add))
                step(nc.vector.tensor_reduce(max_c[:, :, :], pc, AX.X, ALU.max))
                nc.vector.tensor_tensor(pc, pc, per_key(max_c), ALU.subtract).then_inc(S["cs_sub"], 1)

            def cmp_weights(i):
                def go():
                    dve.wait_ge(S["cs_exp"], c.cs_exp.more())
                    step(nc.vector.tensor_reduce(coef_c[:, :, :], pc, AX.X, ALU.add))
                    step(nc.vector.reciprocal(coef_c[:, :, :], coef_c[:, :, :]))
                    gates = branch_gate[:, :, 0, bass.ds(i * GROUP, GROUP)].rearrange("p t u -> p u t")
                    step(nc.vector.tensor_tensor(coef_c[:, :, :], coef_c[:, :, :], gates, ALU.mult))
                    step(nc.vector.tensor_tensor(pc, pc, per_query(cmp_valid), ALU.mult))
                    step(nc.vector.tensor_tensor(pc, pc, per_key(coef_c), ALU.mult))
                return go

            early = p_sc[:, 0:SEQ].rearrange("p (n s) -> p n s", n=2)
            late = p_sc[:, SEQ:3 * SEQ].rearrange("p (n s) -> p n s", n=2)

            def maxima():
                dve.wait_ge(S["qk_ready"], c.qk_ready.more())
                tri = causal_bias[:, P:SEQ].rearrange("p (a s) -> p a s", a=1).broadcast_to([P, 2, P])
                both = causal_bias[:, :].rearrange("p (a s) -> p a s", a=1).broadcast_to([P, 2, SEQ])
                nc.vector.tensor_tensor(early, mix[0][:, 0:SEQ].rearrange("p (n s) -> p n s", n=2), tri, ALU.add)
                step(nc.vector.tensor_tensor(late, mix[1][:, :].rearrange("p (n s) -> p n s", n=2), both, ALU.add))
                nc.vector.tensor_reduce(nmax[:, 0, :], early, AX.X, ALU.max, negate=True)
                nc.vector.tensor_reduce(nmax[:, 1, :], late, AX.X, ALU.max, negate=True).then_inc(
                    S["nmax_ready"], 1)

            def weights(i, u):
                def go():
                    dve.wait_ge(S["p_exp"], c.p_exp.more())
                    step(nc.vector.reciprocal(coef[:, :, :], coef[:, :, :]))
                    gates = branch_gate[:, :, 1:3, bass.ds(i * GROUP + u, 1)].rearrange("p t n a -> p t (n a)")
                    step(nc.vector.tensor_tensor(coef[:, :, :], coef[:, :, :], gates, ALU.mult))
                    for t, part, width in ((0, early, P), (1, late, SEQ)):
                        by = coef[:, t, :].rearrange("p (n a) -> p n a", a=1).broadcast_to([P, 2, width])
                        end = nc.vector.tensor_tensor(part, part, by, ALU.mult)
                    end.then_inc(S["p_ready"], 1)
                return go

            def store_p():
                c.tp_ready0.more()
                dve.wait_ge(S["tp_ready1"], c.tp_ready1.more())
                nc.vector.tensor_copy(p_T[:, 1, 0:3 * P], tp[1][:, 0:3 * P])
                nc.vector.tensor_copy(p_T[0:NCMP, 1, 3 * P:4 * P], tp[1][0:NCMP, 3 * P:4 * P]).then_inc(
                    S["tp_free1"], 1)

            def merge_gate():
                dve.wait_ge(S["acc_free0"], c.acc_free0.more(2))

            c.acc_free0.more(2 * (1 + 2 + 2))
            stored()
            dve.wait_ge(S["branch_gate_ready"], 1)
            with c.loop(dve, KV_HEADS, **dict(LOOP2, tp_ready0=4, tp_ready1=4, cs_ready=1, cs_exp=1, qk_ready=4,
                                              p_exp=4, acc_free0=2, dve_step=2 + 5 + 4 + 8)) as i:
                nc.vector.tensor_scalar(q_st[:, :, :], nq_T[:, i, :, :], float(HD) ** -0.5, None,
                                        ALU.mult).then_inc(S["q_st_ready"], 1)
                nc.vector.tensor_copy(v_st[:, :, :, :].rearrange("p n t d -> p (n t) d"),
                                      vsw[:, :, :, bass.ds(i * HD, HD)].rearrange("p n t d -> p (n t) d"))
                nc.vector.tensor_copy(vc_st[:, :], v_cmp[:, i, :]).then_inc(S["v_st_ready"], 1)
                blocks(first=1, hooks={1: [cmp_max, maxima], 2: [cmp_weights(i)], 3: [weights(i, 0)],
                                       4: [store_p, maxima], 6: [weights(i, 1)], 7: [store_p, maxima]})
                blocks(hooks={1: [weights(i, 2)], 2: [store_p, maxima], 4: [weights(i, 3)], 5: [store_p]})
                summed()
                merge_gate()
                for t in range(NT):
                    nc.vector.tensor_tensor(merged[:, i, t, :], acc[1][t][:, :], gate[:, t, :],
                                            ALU.mult).then_inc(S["acc_free1"], 1)
                blocks(1)

            c.acc_free1.more(2 * (1 + 2 + 2 + 4))

            def on_chunk(n):
                def go():
                    dve.wait_ge(S["on_hi_ready"], n + 1)
                    nc.vector.tensor_tensor(on_lo[:, 4 * n:4 * n + 4, :], on_T[:, n, :, :],
                                            f32(on_hi[:, 4 * n:4 * n + 4, :]), ALU.subtract).then_inc(
                                                S["on_lo_ready"], 1)
                return go

            blocks(2, first=1)
            for begin, trips in ((0, 1), (1, 2), (3, 1)):
                with c.loop(dve, trips, **dict(LOOP2, tp_ready0=1, tp_ready1=1, tp_hi=2, acc_free0=2, acc_free1=2)) as i:
                    part = begin if trips == 1 else i + begin
                    blocks(first=2, hooks={(2, 3, 5, 6)[n]: [on_chunk(n)] for n in range(4)} if begin == 0 else {})
                    blocks()
                    summed()
                    merge_gate()
                    for t in range(NT):
                        nc.vector.tensor_tensor(gate[:, t, :], acc[1][t][:, :], gate[:, t, :],
                                                ALU.mult).then_inc(S["acc_free1"], 1)
                    dve.wait_ge(S["acc_free1"], c.acc_free1.more(2))
                    staging_free()
                    for t in range(NT):
                        nc.vector.tensor_tensor(staging[:, t, :], gate[:, t, :], merged[:, part, t, :],
                                                ALU.add).then_inc(S["staging_full"], 1)
                    blocks(2)
                    tp_split(blocks_of(m_hi)[:, part, :, :], blocks_of(m_lo)[:, part, :, :])

            def row_norms():
                sum_waits(4 * NT)
                step(nc.vector.tensor_reduce(rs_t[:, :], sumsq[:, :, :], AX.X, ALU.add))
                mean_squares(rs_t[:, :], D)
                reciprocal_root()

            dve.wait_ge(S["xres_landed"], 16 * NT)
            for i in range(4):
                blocks(first=2 if i == 0 else 1)
                summed()
                staging_free()
                for t in range(NT):
                    nc.vector.tensor_tensor(staging[:, t, :], acc[i % 2][t][:, :], x1[:, t, i * COL:(i + 1) * COL],
                                            ALU.add).then_inc(S["staging_full"], 1)
                if i == 3:
                    row_norms()
                    nc.vector.tensor_copy(rs_t[:, :], rs[:, :]).then_inc(S["rs_ready"], 1)
                blocks(1)
                tp_split(blocks_of(f_hi)[:, i, :, :], blocks_of(f_lo)[:, i, :, :],
                         lambda f: par[:, C_GFFN + 4 * i + f:C_GFFN + 4 * i + f + 1])

            with c.loop(dve, FFB, **dict(LOOP2, tp_ready0=1, tp_ready1=1, tp_hi=2, gate_ready=2)) as i:
                blocks(first=1)
                dve.wait_ge(S["gate_ready"], c.gate_ready.more(2))
                for t in range(NT):
                    nc.vector.scalar_tensor_tensor(ffn_gate[:, t, :], acc[0][t][:, :], rs[:, t:t + 1],
                                                   ffn_gate[:, t, :], ALU.mult, ALU.mult).then_inc(S["acc_free0"], 1)
                blocks()
                summed()
                staging_free()
                for t in range(NT):
                    nc.vector.scalar_tensor_tensor(staging[:, t, :], acc[1][t][:, :], rs[:, t:t + 1],
                                                   ffn_gate[:, t, :], ALU.mult, ALU.mult).then_inc(
                                                       S["staging_full"], 1)
                blocks(1)
                tp_split(act_hi[:, :, :].rearrange("p (a f) s -> p a f s", f=4)[:, i, :, :],
                         act_lo[:, :, :].rearrange("p (a f) s -> p a f s", f=4)[:, i, :, :])
            for n in range(4):
                blocks(NDOWN, first=1 if n == 0 else 0, splits=NDOWN if n < 3 else NDOWN - LEAD)
                summed()
                for t in range(NT):
                    part = x1[:, t, n * COL:(n + 1) * COL]
                    nc.vector.tensor_tensor(part, acc[n % 2][t][:, :], part, ALU.add).then_inc(
                        S[f"acc_free{n % 2}"], 1)
            row_norms()
            dve.wait_ge(S["gfin_landed"], 16)
            for t in range(NT):
                for half in (slice(0, D // 2), slice(D // 2, D)):
                    nc.vector.scalar_tensor_tensor(x1[:, t, half], x1[:, t, half], rs[:, t:t + 1],
                                                   g_fin_bc[:, half], ALU.mult, ALU.mult).then_inc(S["y_ready"], 1)


def stream_blocks(w, k_tiles, cols):
    k, n = w.shape
    v = w.reshape(k // (k_tiles * P), k_tiles, P, n // cols, cols)
    return v.transpose(3, 0, 2, 1, 4).reshape(-1, P, k_tiles * cols)


def kernel(x, g_mix, w_in, w_gla_gate, b_gla_gate, g_gla_out, pe_cmp_k, w_cmp_k1, w_cmp_k2, pe_cmp_v, w_cmp_v1,
           w_cmp_v2, w_proj_gla, w_proj_nsa, w_out, g_ffn, w_ffn_gate, w_ffn_up, w_ffn_down, g_final):
    import concourse.bacc as bacc
    from concourse.bass_utils import run_bass_kernel_spmd

    def column_blocks(w):
        return stream_blocks(w, KSB, COL).reshape(w.shape[1] // COL, -1, P, SB)

    w_in = np.asarray(w_in)[0]
    kv = column_blocks(w_in[:, O_KV:O_NG])
    gates = column_blocks(w_in[:, O_MG:])
    p_gla, p_nsa = column_blocks(np.asarray(w_proj_gla)[0]), column_blocks(np.asarray(w_proj_nsa)[0])
    f_gate, f_up = column_blocks(np.asarray(w_ffn_gate)[0]), column_blocks(np.asarray(w_ffn_up)[0])
    parts = [kv[0], kv[1], kv[2], kv[4], kv[3], kv[5],
             stream_blocks(np.asarray(w_cmp_k1)[0], 4, CMP_HIDDEN),
             stream_blocks(np.asarray(w_cmp_v1)[0], 4, CMP_HIDDEN),
             *column_blocks(w_in[:, O_GQ:O_LR]), *column_blocks(w_in[:, O_NQ:O_KV])]
    for i in range(4):
        parts += [gates[i], p_gla[i]]
    for i in range(4):
        parts += [gates[4 + i], p_nsa[i]]
    parts += [*column_blocks(np.asarray(w_out)[0])]
    for i in range(FFB):
        parts += [f_gate[i], f_up[i]]
    parts += [*column_blocks(np.asarray(w_ffn_down)[0])]
    stream = np.concatenate(parts)
    assert stream.shape[0] == STREAM

    def by_feature(v):
        return np.asarray(v).reshape(-1, P).T

    params = np.concatenate([by_feature(g_mix), by_feature(g_ffn), by_feature(b_gla_gate),
                             np.asarray(pe_cmp_k)[0].T, np.asarray(pe_cmp_v)[0].T], axis=1)
    small = np.concatenate([w_in[:, O_LR:O_NQ], w_in[:, O_NG:O_MG]], axis=1)
    w2 = np.stack([np.asarray(w)[0].reshape(2, P, HD) for w in (w_cmp_k2, w_cmp_v2)])
    arrays = {
        "wstream": stream,
        "x": np.asarray(x).reshape(NT, P, D),
        "params": params,
        "wsmall": small.reshape(KT, P, NSMALL).transpose(1, 0, 2),
        "w_gate": np.asarray(w_gla_gate)[0],
        "w2": w2.transpose(2, 0, 1, 3),
        "g_gla": np.asarray(g_gla_out).reshape(1, HV),
        "g_final": np.asarray(g_final).reshape(1, D),
    }
    arrays = {n: np.ascontiguousarray(a) for n, a in arrays.items()}
    nc = bacc.Bacc("TRN2", target_bir_lowering=False, num_devices=1)
    args = [nc.dram_tensor(n, a.shape, F32, kind="ExternalInput").ap() for n, a in arrays.items()]
    out = nc.dram_tensor("out", (NT, P, D), F32, kind="ExternalOutput").ap()
    build(nc, *args, out)
    r = run_bass_kernel_spmd(nc, [arrays], core_ids=[0])
    return r.results[0]["out"].reshape(1, SEQ, D)
```
